# Optimizing a Trainium2 kernel written in Bass

```python
import jax, jax.numpy as jnp
from jax import lax
import numpy as np

D_MODEL = 1024
BATCH = 1
SEQ = 256
DEPTH = 2

HEAD_DIM = 64
D_ATTN = D_MODEL // 2
N_Q_HEADS = D_ATTN // HEAD_DIM
N_KV_HEADS = 2
Q_PER_KV = N_Q_HEADS // N_KV_HEADS
D_KV = N_KV_HEADS * HEAD_DIM
D_FOURIER = D_MODEL - D_ATTN
N_FOURIER_GROUPS = 8
FOURIER_GROUP = D_FOURIER // N_FOURIER_GROUPS
D_IN = D_ATTN + 2 * D_KV + D_FOURIER
D_MIX = D_ATTN + D_FOURIER
WINDOW = 128
BLOCK = 128
ROPE_THETA = 500000.0
ROT_DIM = HEAD_DIM // 4
D_FF = 3584
N_EXPERTS = 8
TOP_K = 2
EPS = 1e-6
N_DENSE = (DEPTH + 1) // 2
N_MOE = DEPTH // 2

kernel_name = "hybrid_swa_fnet_moe_encoder"

def rmsnorm(x, g):
    xf = x.astype(jnp.float32)
    y = xf * lax.rsqrt(jnp.mean(xf * xf, axis=-1, keepdims=True) + EPS)
    return (y * g.astype(jnp.float32)).astype(x.dtype)

def rope_partial(x, cos, sin):
    half = ROT_DIM // 2
    x1 = x[..., :half]
    x2 = x[..., half:ROT_DIM]
    rot = jnp.concatenate([x1 * cos - x2 * sin, x2 * cos + x1 * sin], axis=-1)
    return jnp.concatenate([rot, x[..., ROT_DIM:]], axis=-1)

def banded_sink_attention(q, k, v, sink):
    B, S = q.shape[0], q.shape[1]
    nb = S // BLOCK
    qb = q.reshape(B, nb, BLOCK, N_KV_HEADS, Q_PER_KV, HEAD_DIM)

    def band(t):
        tp = jnp.pad(t, ((0, 0), (BLOCK, BLOCK), (0, 0), (0, 0)))
        tp = tp.reshape(B, nb + 2, BLOCK, N_KV_HEADS, HEAD_DIM)
        return jnp.concatenate([tp[:, :-2], tp[:, 1:-1], tp[:, 2:]], axis=2)

    kb, vb = band(k), band(v)
    scores = jnp.einsum('bnqhgd,bnkhd->bnhgqk', qb, kb).astype(jnp.float32) * (HEAD_DIM ** -0.5)
    qi = jnp.arange(BLOCK)[:, None]
    kj = jnp.arange(3 * BLOCK)[None, :]
    blk = jnp.arange(nb)[:, None, None]
    k_abs = blk * BLOCK - BLOCK + kj
    mask = (jnp.abs(kj - BLOCK - qi) <= WINDOW) & (k_abs >= 0) & (k_abs < S)
    scores = jnp.where(mask[None, :, None, None], scores, -jnp.inf)
    sink_b = sink.astype(jnp.float32).reshape(N_KV_HEADS, Q_PER_KV)[None, None, :, :, None, None]
    m = jnp.maximum(jnp.max(scores, axis=-1, keepdims=True), sink_b)
    p = jnp.exp(scores - m)
    probs = p / (jnp.sum(p, axis=-1, keepdims=True) + jnp.exp(sink_b - m))
    out = jnp.einsum('bnhgqk,bnkhd->bnqhgd', probs.astype(v.dtype), vb)
    return out.reshape(B, S, N_Q_HEADS * HEAD_DIM)

def fourier_mix(f, w_fmix):
    B, S = f.shape[0], f.shape[1]
    fg = f.astype(jnp.float32).reshape(B, S, N_FOURIER_GROUPS, FOURIER_GROUP)
    spec = jnp.fft.fft2(fg, axes=(1, 3), norm="ortho").real.astype(f.dtype)
    return jnp.einsum('bsgc,gcd->bsgd', spec, w_fmix).reshape(B, S, D_FOURIER)

def swiglu(h, w_gate, w_up, w_down):
    return (jax.nn.silu(h @ w_gate) * (h @ w_up)) @ w_down

def moe_swiglu(h, w_router, e_gate, e_up, e_down):
    B, S, D = h.shape
    t = h.reshape(B * S, D)
    logits = (t @ w_router).astype(jnp.float32)
    top_vals, top_idx = lax.top_k(logits, TOP_K)
    top_w = jax.nn.softmax(top_vals, axis=-1)
    gates = jnp.sum(jax.nn.one_hot(top_idx, N_EXPERTS, dtype=jnp.float32) * top_w[..., None], axis=1)
    out = jnp.zeros_like(t)
    for e in range(N_EXPERTS):
        out = out + gates[:, e:e + 1].astype(t.dtype) * swiglu(t, e_gate[e], e_up[e], e_down[e])
    return out.reshape(B, S, D)

def setup_inputs(seed: int = 0) -> dict:
    key = jax.random.key(seed)
    ks = jax.random.split(key, 20)
    f32 = jnp.float32

    def nrm(k, shape, scale):
        return jax.random.normal(k, shape, f32) * scale

    def gain(k, shape):
        return 1.0 + 0.1 * jax.random.normal(k, shape, f32)

    offsets = jax.random.randint(ks[1], (BATCH, 1), 0, 1024, dtype=jnp.int32)
    positions = jnp.arange(SEQ, dtype=jnp.int32)[None, :] + offsets
    return {
        "x": jax.random.normal(ks[0], (BATCH, SEQ, D_MODEL), f32),
        "positions": positions,
        "norm_mix": gain(ks[2], (DEPTH, D_MODEL)),
        "w_in": nrm(ks[3], (DEPTH, D_MODEL, D_IN), D_MODEL ** -0.5),
        "q_norm": gain(ks[4], (DEPTH, HEAD_DIM)),
        "k_norm": gain(ks[5], (DEPTH, HEAD_DIM)),
        "sink": nrm(ks[6], (DEPTH, N_Q_HEADS), 0.5),
        "w_fmix": nrm(ks[7], (DEPTH, N_FOURIER_GROUPS, FOURIER_GROUP, FOURIER_GROUP), FOURIER_GROUP ** -0.5),
        "g_attn_out": gain(ks[8], (DEPTH, D_ATTN)),
        "g_fourier_out": gain(ks[9], (DEPTH, D_FOURIER)),
        "w_out": nrm(ks[10], (DEPTH, D_MIX, D_MODEL), D_MIX ** -0.5),
        "norm_ffn": gain(ks[11], (DEPTH, D_MODEL)),
        "ffn_gate": nrm(ks[12], (N_DENSE, D_MODEL, D_FF), D_MODEL ** -0.5),
        "ffn_up": nrm(ks[13], (N_DENSE, D_MODEL, D_FF), D_MODEL ** -0.5),
        "ffn_down": nrm(ks[14], (N_DENSE, D_FF, D_MODEL), D_FF ** -0.5),
        "w_router": nrm(ks[15], (N_MOE, D_MODEL, N_EXPERTS), D_MODEL ** -0.5),
        "e_gate": nrm(ks[16], (N_MOE, N_EXPERTS, D_MODEL, D_FF), D_MODEL ** -0.5),
        "e_up": nrm(ks[17], (N_MOE, N_EXPERTS, D_MODEL, D_FF), D_MODEL ** -0.5),
        "e_down": nrm(ks[18], (N_MOE, N_EXPERTS, D_FF, D_MODEL), D_FF ** -0.5),
    }

def reference(x, positions, norm_mix, w_in, q_norm, k_norm, sink, w_fmix, g_attn_out, g_fourier_out,
              w_out, norm_ffn, ffn_gate, ffn_up, ffn_down, w_router, e_gate, e_up, e_down):
    B, S = x.shape[0], x.shape[1]
    inv_freq = ROPE_THETA ** (-jnp.arange(0, ROT_DIM, 2, dtype=jnp.float32) / ROT_DIM)
    ang = positions.astype(jnp.float32)[..., None] * inv_freq
    cos = jnp.cos(ang)[:, :, None, :].astype(x.dtype)
    sin = jnp.sin(ang)[:, :, None, :].astype(x.dtype)

    for l in range(DEPTH):
        h = rmsnorm(x, norm_mix[l])
        z = h @ w_in[l]
        q = z[..., :D_ATTN].reshape(B, S, N_Q_HEADS, HEAD_DIM)
        k = z[..., D_ATTN:D_ATTN + D_KV].reshape(B, S, N_KV_HEADS, HEAD_DIM)
        v = z[..., D_ATTN + D_KV:D_ATTN + 2 * D_KV].reshape(B, S, N_KV_HEADS, HEAD_DIM)
        f = z[..., D_ATTN + 2 * D_KV:]
        q = rope_partial(rmsnorm(q, q_norm[l]), cos, sin)
        k = rope_partial(rmsnorm(k, k_norm[l]), cos, sin)
        a = banded_sink_attention(q, k, v, sink[l])
        fo = fourier_mix(f, w_fmix[l])
        mixed = jnp.concatenate([rmsnorm(a, g_attn_out[l]), rmsnorm(fo, g_fourier_out[l])], axis=-1)
        x = x + mixed @ w_out[l]
        h = rmsnorm(x, norm_ffn[l])
        i = l // 2
        if l % 2 == 0:
            x = x + swiglu(h, ffn_gate[i], ffn_up[i], ffn_down[i])
        else:
            x = x + moe_swiglu(h, w_router[i], e_gate[i], e_up[i], e_down[i])
    return x


_drawn_inputs = setup_inputs


def setup_inputs(seed=0):
    import zlib

    import numpy as np

    out = dict(_drawn_inputs(seed))
    spreads = {}
    factors = {'sink': 8.0}
    for name, (base, spread) in spreads.items():
        noise = np.random.default_rng([zlib.crc32(name.encode()), seed]).standard_normal(out[name].shape)
        drawn = base * np.exp(spread * noise) if base else spread * noise
        out[name] = __import__('jax').numpy.asarray(drawn.astype(out[name].dtype))
    for name, factor in factors.items():
        out[name] = (out[name] * factor).astype(out[name].dtype)
    return out
```

```python
from contextlib import ExitStack

import concourse.bass as bass
from concourse import mybir

F32 = mybir.dt.float32
F32R = mybir.dt.float32r
I32 = mybir.dt.int32
ALU = mybir.AluOpType
ACT = mybir.ActivationFunctionType
AX_X = mybir.AxisListType.X

P = 128
SEQ, D, DEPTH = 256, 1024, 2
TT = SEQ // P
KD = D // P
HEAD, NQ, NKV = 64, 8, 2
QPK = NQ // NKV
DQ, DKV = NQ * HEAD, NKV * HEAD
DA = DF = D // 2
NH = NQ + NKV
DIN = DQ + 2 * DKV + DF
V0, FO0 = DQ + DKV, DQ + 2 * DKV
HALF = 8
FF, NE = 3584, 8
JF = FF // 512
EPS = 1e-6
SCALE = HEAD ** -0.5
MAXJ = 16

GW = 2048
RAW, SPL = 6, 3
MIXG = 9
JOBG = 6 * JF

C_ID = 0
C_MASK = C_ID + P
C_CS = C_MASK + TT * SEQ
C_CC = C_CS + TT * 2 * SEQ
C_SC = C_CC + P
C_U = C_SC + P
C_ONE = C_U + P
C_IOTA = C_ONE + P
C_LT = C_IOTA + P
C_FREQ = C_LT + NE * NE
C_JOB = C_FREQ + HALF
C_PIDX = C_JOB + MAXJ
C_N = C_PIDX + 1

TWO_PI = 6.283185307179586
PI_1 = 6.28125
PI_2 = 0.0019350051879882812
PI_3 = TWO_PI - PI_1 - PI_2
ROUND = 12582912.0
PI_SAFE = 3.1415925


def build_trunk(nc, x, positions, norm_mix, w_in, q_norm, k_norm, sink, w_fmix, g_attn_out,
                g_fourier_out, w_out, norm_ffn, ffn_gate, ffn_up, ffn_down, w_router,
                e_gate, e_up, e_down, consts, out):
    with ExitStack() as ctx:
        def sb(name, shape, dt=F32):
            return ctx.enter_context(nc.sbuf_tensor(name, shape, dt))

        def sem(name):
            return ctx.enter_context(nc.semaphore(name))

        raw = sb("raw", [P, RAW, GW])
        whi = sb("whi", [P, SPL, GW], F32R)
        wlo = sb("wlo", [P, SPL, GW], F32R)
        xs = sb("xs", [P, TT, D])
        hs = sb("hs", [P, TT, D])
        hThi = sb("hThi", [P, KD, SEQ], F32R)
        hTlo = sb("hTlo", [P, KD, SEQ], F32R)
        zs = sb("zs", [P, TT, DIN])
        probs = sb("probs", [P, NKV, QPK, TT, SEQ])
        probsT = sb("probsT", [P, QPK, 2, TT, P])
        posT = sb("posT", [P, 4, 2 * SEQ])
        fmixA = sb("fmixA", [P, 2, DF])
        fmixW = sb("fmixW", [P, 4, P])
        cst = sb("cst", [P, C_N])
        gain1 = sb("gain1", [P, D])
        gain2 = sb("gain2", [P, D])
        qkgain = sb("qkgain", [P, NH, HEAD])
        sinks = sb("sinks", [P, NQ])
        actThi = sb("actThi", [P, TT, 4, P], F32R)
        actTlo = sb("actTlo", [P, TT, 4, P], F32R)
        small = sb("small", [P, 640])
        posi = sb("posi", [P, TT], I32)
        jobtab = sb("jobtab", [1, MAXJ + 1], I32)

        pflat = probs[:].rearrange("p a b c d -> p (a b c d)")
        actg = pflat[:, 0:1024].rearrange("p (t f) -> p t f", t=TT)
        ysb = pflat[:, 1024:2048]
        rows = pflat[:, 2048:3072].rearrange("p (c s) -> p c s", c=4)
        selG = pflat[:, 3072:3328].rearrange("p (t s) -> p t s", t=TT)
        selS = pflat[:, 3328:3584]
        tmpS = pflat[:, 3584:3840]
        diag = pflat[:, 0:1024].rearrange("p (c s) -> p c s", c=8)
        cmp1 = pflat[:, 3072:3200].rearrange("p (t a b) -> p t a b", t=TT, a=NE)
        cmp2 = pflat[:, 3200:3328].rearrange("p (t a b) -> p t a b", t=TT, a=NE)
        lgT = pflat[0:NE, 3328:3584]
        iota = pflat[:, 3840:3968]
        tflat = probsT[:].rearrange("p a b c d -> p (a b c d)")
        qks = tflat[:, 0:TT * NH * HEAD].rearrange("p (t n) -> p t n", t=TT)
        wr = posT[:].rearrange("p a b -> p (a b)")[:, 0:KD * NE].rearrange("p (k e) -> p k e", k=KD)
        xThi = hThi[:].rearrange("p k s -> p (k s)")[:, 0:KD * P].rearrange("p (k s) -> p k s", k=KD)
        xTlo = hTlo[:].rearrange("p k s -> p (k s)")[:, 0:KD * P].rearrange("p (k s) -> p k s", k=KD)

        at = [0]

        def cols(n, *dims):
            a = small[:, at[0]:at[0] + n]
            at[0] += n
            if len(dims) == 2:
                a = a.rearrange("p (a b) -> p a b", a=dims[0])
            if len(dims) == 3:
                a = a.rearrange("p (a b c) -> p a b c", a=dims[0], b=dims[1])
            return a

        eps = cols(1)
        ss = cols(TT)
        ssm = cols(2 * TT, TT, 2)
        cos = cols(TT * HALF, TT, HALF)
        sin = cols(TT * HALF, TT, HALF)
        ang = cols(TT * HALF, TT, HALF)
        ang2 = cols(TT * HALF, TT, HALF)
        posf = cols(TT)
        qss = cols(TT * NH, TT, NH)
        mx = cols(NKV * QPK * TT, NKV, QPK, TT)
        negm = cols(NKV * QPK * TT, NKV, QPK, TT)
        esink = cols(NKV * QPK * TT, NKV, QPK, TT)
        rsum = cols(NKV * QPK * TT, NKV, QPK, TT)
        lg = cols(TT * NE, TT, NE)
        rank = cols(TT * NE, TT, NE)
        pick = cols(2 * TT * NE, 2, TT, NE)
        pickv = cols(2 * TT * NE, 2, TT, NE)
        both = cols(TT * NE, TT, NE)
        lc = cols(2 * TT, 2, TT)
        e2 = cols(TT)
        e1 = cols(TT)
        gate = cols(2 * TT, 2, TT)
        gslot = cols(2 * TT, 2, TT)
        posc = cols(3 * NE, 3, NE)
        jobs = cols(NE)
        jobs2 = cols(NE)
        jbase = cols(NE)
        jend = cols(NE)
        jexp = cols(MAXJ + 1)
        sidx = cols(1)
        assert at[0] <= 640
        rtmp = [pflat[:, i * 160:(i + 1) * 160]
                .rearrange("p (t h d) -> p t h d", t=TT, h=NH) for i in range(4)]

        ident = cst[:, C_ID:C_ID + P]
        mask = cst[:, C_MASK:C_MASK + TT * SEQ]
        dft = cst[:, C_CS:C_CS + TT * 2 * SEQ].rearrange("p (t n) -> p t n", t=TT)
        ones = cst[:, C_ONE:C_ONE + P]
        upper = cst[:, C_U:C_U + P]
        ltri = cst[:, C_LT:C_LT + NE * NE].rearrange("p (a b) -> p a b", a=NE)

        bank = [ctx.enter_context(nc.psum_tensor(f"bank{i}", [P, 512], F32)) for i in range(8)]

        in_x, in_c, in_p, in_gain, in_mix, in_gain2, in_wr = (sem("x_loaded"), sem("consts_loaded"), sem("positions_loaded"), sem("gain1_loaded"),
                                          sem("mix_params_loaded"), sem("gain2_loaded"), sem("router_loaded"))
        landed = [sem(f"granule_landed{i}") for i in range(RAW)]
        hi_ready, lo_ready, w_used = sem("w_hi_ready"), sem("w_lo_ready"), sem("w_used")
        link_s = sem("dve_step")
        eps_set, fmix_zero = sem("eps_set"), sem("fmixw_zeroed")
        sq_s, std_s, h_s, hTp_s, hThi_s, hTlo_s = (sem("squares"), sem("std"), sem("h_ready"), sem("hT_in_psum"),
                                                   sem("hT_hi"), sem("hT_lo"))
        zc_s = sem("z_copied")
        trig_in, trig_s = sem("trig_args"), sem("trig_ready")
        fA_s, fAc_s = sem("fmixA_in_psum"), sem("fmixA_copied")
        pos_s, posc_s = sem("posT_in_psum"), sem("posT_copied")
        qss_s, qstd_s, qk_s = sem("qk_squares"), sem("qk_std"), sem("qk_ready")
        qT_s, qTc_s = sem("qT_in_psum"), sem("qT_copied")
        sc_s, scm_s, mx_s, exp_s = sem("scores"), sem("scores_masked"), sem("row_max"), sem("exps")
        pT_s, pTa_s, pTd_s = sem("probsT_in_psum"), sem("probsT_copied_act"), sem("probsT_copied_dve")
        o_s, a_s = sem("pv_in_psum"), sem("attn_ready")
        fo_s, foc_s = sem("fourier_in_psum"), sem("fourier_copied")
        msq_s, mstd_s = sem("mixed_squares"), sem("mixed_std")
        wo_s, x_s = sem("branch_in_psum"), sem("x_updated")

        class Ffn:
            pass

        def ffn_sems(tag):
            f = Ffn()
            f.gate, f.silu, f.up, f.act = (sem(tag + "gate_in_psum"), sem(tag + "silu"), sem(tag + "up_in_psum"),
                                           sem(tag + "act_ready"))
            f.T, f.hi, f.lo, f.y = (sem(tag + "actT_in_psum"), sem(tag + "actT_hi"), sem(tag + "actT_lo"),
                                    sem(tag + "down_in_psum"))
            return f

        dn, mo = ffn_sems("d_"), ffn_sems("m_")
        wrc_s, wrz_s, wrl_s = sem("router_hi"), sem("router_zeroed"), sem("router_lo")
        lg_s, lgc_s, lt_s = sem("logitsT_in_psum"), sem("logitsT_copied"), sem("logits_in_psum")
        d_s, e_s, cnt_s, diag_s, row_s, rowc_s = (
            sem("choices_and_gap"), sem("exp_of_sink_or_gap"), sem("counts_in_psum"), sem("diag_ready"),
            sem("rows_in_psum"), sem("rows_copied"))
        job_s = sem("jobs_ready")
        sel_s, gth_s, xhi_s, xlo_s = sem("sel_ready"), sem("gathered"), sem("job_x_hi"), sem("job_x_lo")
        gst_s, yc_s, sca_s, xadd_s = sem("gated_sel_ready"), sem("y_copied"), sem("scattered"), sem("x_added")
        yz_s = sem("y_zeroed")
        out_s = sem("out_stored")

        block = ctx.enter_context(nc.Block())

        mix_base = [0, MIXG + JOBG]
        dense_base = MIXG
        moe_base = 2 * MIXG + JOBG
        assert moe_base % RAW == 0 and MIXG % SPL == 0 and JOBG % RAW == 0

        @block.sync
        def _(sp):
            sp.dma_start(xs[:, 0, :], x[0, 0:P, :]).then_inc(in_x, 16)
            sp.dma_start(xs[:, 1, :], x[0, P:SEQ, :]).then_inc(in_x, 16)
            sp.dma_start(cst[:], consts).then_inc(in_c, 16)

            def slot_free(g):
                sp.wait_ge(lo_ready, g - RAW + 1)

            def put(g, slot, src, width=GW):
                dst = raw[:, slot, 0:width]
                if len(src.shape) == 3:
                    dst = dst.rearrange("p (k f) -> p k f", k=src.shape[1])
                sp.dma_start(dst, src).then_inc(landed[slot], 16)

            def mix(l):
                b = mix_base[l]
                wi = w_in[l].rearrange("(k p) n -> p k n", p=P)
                wo = w_out[l].rearrange("(k p) n -> p k n", p=P)
                srcs = [wi[:, 4 * h:4 * h + 4, 512 * c:512 * c + 512] for c in range(2) for h in range(2)]
                srcs += [wi[:, :, 1024:DIN]]
                srcs += [wo[:, 4 * h:4 * h + 4, 512 * c:512 * c + 512] for c in range(2) for h in range(2)]
                for i, s in enumerate(srcs):
                    if b + i >= RAW:
                        slot_free(b + i)
                    put(b + i, (b + i) % RAW, s)

            def ffn(base, slot0, wg, wu, wd):
                def up_gran(w, j, h):
                    return w[:, 4 * h:4 * h + 4, bass.ds(j * 512, 512)]

                def down_gran(j, h):
                    return wd[:, bass.ds(j * 4 + 2 * h, 2), :]

                for i, s in enumerate([up_gran(wg, 0, 0), up_gran(wg, 0, 1), up_gran(wu, 0, 0), up_gran(wu, 0, 1)]):
                    slot_free(base + i)
                    put(base + i, (slot0 + i) % RAW, s)
                with sp.Fori(0, JF - 1) as j:
                    for c in range(6):
                        slot_free(base + 4 + j * 6 + c)
                        s = [up_gran(wg, j + 1, 0), up_gran(wg, j + 1, 1), down_gran(j, 0), down_gran(j, 1),
                             up_gran(wu, j + 1, 0), up_gran(wu, j + 1, 1)][c]
                        put(None, (slot0 + 4 + c) % RAW, s)
                for h in range(2):
                    slot_free(base + JOBG - 2 + h)
                    put(None, (slot0 + JOBG - 2 + h) % RAW, down_gran(JF - 1, h))

            mix(0)
            ffn(dense_base, dense_base, ffn_gate[0].rearrange("(k p) n -> p k n", p=P),
                ffn_up[0].rearrange("(k p) n -> p k n", p=P), ffn_down[0].rearrange("(k p) n -> p k n", p=P))
            mix(1)
            sp.wait_ge(job_s, 1)
            njobs = sp.value_load(jobtab[0:1, MAXJ:MAXJ + 1], min_val=1, max_val=MAXJ)
            with sp.Fori(0, njobs) as n:
                e = sp.value_load(jobtab[0:1, bass.ds(n, 1)], min_val=0, max_val=NE - 1)

                def of(w):
                    return w[0].rearrange("e (k p) n -> e p k n", p=P)[bass.ds(e, 1)].rearrange("e p k n -> (e p) k n")
                ffn(n * JOBG + moe_base, moe_base, of(e_gate), of(e_up), of(e_down))
            for t in range(TT):
                sp.wait_ge(xadd_s, (njobs + 1) * 4)
                sp.dma_start(out[0, t * P:(t + 1) * P, :], xs[:, t, :]).then_inc(out_s, 16)
            sp.wait_ge(out_s, 16 * TT)

        @block.gpsimd
        def _(pool):
            nc.gpsimd.memset(eps, EPS).then_inc(eps_set, 1)
            nc.gpsimd.memset(fmixW[:], 0.0).then_inc(fmix_zero, 1)
            for t in range(TT):
                pool.dma_start(posi[:, t:t + 1], positions[0, t * P:(t + 1) * P].rearrange("(p o) -> p o", o=1)).then_inc(in_p, 16)
            pool.wait_ge(fmix_zero, 1)

            def mix_params(l):
                pool.dma_start(qkgain[:, 0:NQ, :], q_norm[l].partition_broadcast(P).unsqueeze(1)
                               .broadcast_to([P, NQ, HEAD])).then_inc(in_mix, 16)
                pool.dma_start(qkgain[:, NQ:NH, :], k_norm[l].partition_broadcast(P).unsqueeze(1)
                               .broadcast_to([P, NKV, HEAD])).then_inc(in_mix, 16)
                pool.dma_start(sinks[:], sink[l].partition_broadcast(P)).then_inc(in_mix, 16)
                for a in range(2):
                    pool.dma_start(fmixW[64 * a:64 * a + 64, :, 64 * a:64 * a + 64],
                                   w_fmix[l].rearrange("(c two) i o -> two i c o", two=2)[a]).then_inc(in_mix, 16)

            def gain(g):
                pool.dma_start(gain1[:], g.partition_broadcast(P)).then_inc(in_gain, 16)

            def gains2(l):
                pool.dma_start(gain2[:, 0:DA], g_attn_out[l].partition_broadcast(P)).then_inc(in_gain2, 16)
                pool.dma_start(gain2[:, DA:D], g_fourier_out[l].partition_broadcast(P)).then_inc(in_gain2, 16)

            gain(norm_mix[0])
            mix_params(0)
            gains2(0)
            pool.wait_ge(h_s, TT)
            gain(norm_ffn[0])
            pool.wait_ge(h_s, 2 * TT)
            mix_params(1)
            gains2(1)
            pool.wait_ge(h_s, 3 * TT)
            gain(norm_mix[1])
            pool.wait_ge(h_s, 4 * TT)
            gain(norm_ffn[1])
            pool.wait_ge(foc_s, 2 * TT)
            pool.dma_start(wr, w_router[0].rearrange("(k p) e -> p k e", p=P)).then_inc(in_wr, 16)

        x_need = {0: 0, 2: 4, 3: 8, 5: 12}

        @block.tensor
        def _(pe):
            def mm(o, a, b, start, stop):
                return nc.tensor.matmul(o, a, b, start=start, stop=stop)

            def mm3(o, ahi, alo, bhi, blo, start, stop):
                mm(o, ahi, bhi, start, False)
                mm(o, ahi, blo, False, False)
                return mm(o, alo, bhi, False, stop)

            def block_of(slot, b, width=512):
                return whi[:, slot, b * width:(b + 1) * width], wlo[:, slot, b * width:(b + 1) * width]

            def norm_T(u):
                pe.wait_ge(h_s, u * TT + TT)
                if u:
                    pe.wait_ge(hTlo_s, 4 * u)
                for b in range(4):
                    for kk in range(2):
                        for t in range(TT):
                            k = 2 * b + kk
                            m = nc.tensor.transpose(bank[b][:, kk * SEQ + t * P:kk * SEQ + (t + 1) * P],
                                                    hs[:, t, k * P:(k + 1) * P], ident)
                    m.then_inc(hTp_s, 1)

            def project(g, banks, first, last):
                pe.wait_ge(lo_ready, g + 1)
                for t in range(TT):
                    for b in range(4):
                        k = (0 if first else 4) + b
                        whb, wlb = block_of(g % SPL, b)
                        tok = slice(t * P, (t + 1) * P)
                        m = mm3(bank[banks[t]][:], hThi[:, k, tok], hTlo[:, k, tok], whb, wlb,
                                first and b == 0, last and b == 3)
                m.then_inc(w_used, 1)

            def mix(l):
                base = mix_base[l]
                norm_T(3 * l)
                pe.wait_ge(hTlo_s, 4 * (3 * l) + 4)
                project(base, (4, 5), True, False)
                project(base + 1, (4, 5), False, True)
                project(base + 2, (6, 7), True, False)
                project(base + 3, (6, 7), False, True)
                g = base + 4
                pe.wait_ge(lo_ready, g + 1)
                for t in range(TT):
                    for k in range(KD):
                        whb, wlb = block_of(g % SPL, k, 256)
                        tok = slice(t * P, (t + 1) * P)
                        m = mm3(bank[t][:, 0:256], hThi[:, k, tok], hTlo[:, k, tok], whb, wlb, k == 0, k == KD - 1)
                m.then_inc(w_used, 1)
                if l == 0:
                    pe.wait_ge(in_c, 16)
                pe.wait_ge(in_mix, 80 * (l + 1))
                fw = fmixW[:].rearrange("p a b -> p (a b)")
                mm(bank[2][:], cst[:, C_CC:C_CC + P], fw, True, True)
                mm(bank[3][:], cst[:, C_SC:C_SC + P], fw, True, True).then_inc(fA_s, 1)
                pe.wait_ge(zc_s, 6 * (l + 1))
                for c in range(4):
                    for t in range(TT):
                        m = mm(bank[4 + c][:], zs[:, t, FO0 + c * P:FO0 + (c + 1) * P], dft[:, t, :],
                               t == 0, t == TT - 1)
                    m.then_inc(pos_s, 1)
                pe.wait_ge(qk_s, l + 1)
                pe.wait_ge(fAc_s, 2 * (l + 1))
                for i in range(5):
                    for t in range(TT):
                        m = nc.tensor.transpose(bank[i // 2][:, (i % 2) * SEQ + t * P:(i % 2) * SEQ + (t + 1) * P],
                                                qks[:, t, i * P:(i + 1) * P], ident)
                    if i % 2 or i == 4:
                        m.then_inc(qT_s, 1)
                pe.wait_ge(posc_s, 4 * (l + 1))
                pe.wait_ge(qTc_s, 3 * (l + 1))
                for r in range(NKV):
                    for i in range(QPK):
                        for t in range(TT):
                            rows_ = slice(HEAD * r, HEAD * r + HEAD)
                            m = mm(bank[4 * (1 - r) + i][:, t * SEQ:(t + 1) * SEQ], zs[rows_, t, i * P:(i + 1) * P],
                                   zs[rows_, :, 4 * P:5 * P], True, True)
                        m.then_inc(sc_s, 1)
                for r in range(NKV):
                    if r == 0:
                        pe.wait_ge(scm_s, 8 * l + 4)
                    else:
                        pe.wait_ge(pTa_s, 2 * (2 * l + r))
                        pe.wait_ge(pTd_s, 2 * (2 * l + r))
                    for i in range(QPK):
                        pe.wait_ge(exp_s, 8 * (2 * l + r) + 2 * i + 2)
                        for kt in range(2):
                            for t in range(TT):
                                m = nc.tensor.transpose(bank[4 + i][:, (kt * TT + t) * P:(kt * TT + t + 1) * P],
                                                        probs[:, r, i, t, kt * P:(kt + 1) * P], ident)
                        m.then_inc(pT_s, 1)
                    if r == 0:
                        pe.wait_ge(scm_s, 8 * l + 8)
                    pe.wait_ge(pTa_s, 2 * (2 * l + r + 1))
                    pe.wait_ge(pTd_s, 2 * (2 * l + r + 1))
                    for t in range(TT):
                        for i in range(QPK):
                            for kt in range(2):
                                m = mm(bank[2 * r + t][:, i * HEAD:(i + 1) * HEAD], probsT[:, i, kt, t, :],
                                       zs[:, kt, V0 + r * HEAD:V0 + (r + 1) * HEAD], kt == 0, kt == 1)
                        m.then_inc(o_s, 1)
                pe.wait_ge(a_s, 4 * l + 2)
                for t in range(TT):
                    for c in range(4):
                        mm(bank[t][:, c * P:(c + 1) * P], posT[:, c, t * P:(t + 1) * P],
                           fmixA[:, 0, c * P:(c + 1) * P], True, False)
                        m = mm(bank[t][:, c * P:(c + 1) * P], posT[:, c, SEQ + t * P:SEQ + (t + 1) * P],
                               fmixA[:, 1, c * P:(c + 1) * P], False, True)
                    m.then_inc(fo_s, 1)
                norm_T(3 * l + 1)
                pe.wait_ge(hTlo_s, 4 * (3 * l + 1) + 4)
                project(base + 5, (4, 5), True, False)
                project(base + 6, (4, 5), False, True)
                project(base + 7, (6, 7), True, False)
                project(base + 8, (6, 7), False, True)

            def gate_up(f, tiles, lhi, llo, g, slot, half, to_bank, done):
                pe.wait_ge(lo_ready, g + 1)
                for t in range(tiles):
                    for b in range(4):
                        whb, wlb = block_of(slot, b)
                        m = mm3(bank[to_bank + t][:], lhi(4 * half + b, t), llo(4 * half + b, t), whb, wlb,
                                half == 0 and b == 0, half == 1 and b == 3)
                    if half == 1 and t < tiles - 1:
                        m.then_inc(done, 1)
                m.then_inc(w_used, 1)

            def act_T(f, tiles, step):
                for t in range(tiles):
                    pe.wait_ge(f.act, step * tiles + t + 1)
                    for b in range(4):
                        m = nc.tensor.transpose(bank[2 + t][:, b * P:(b + 1) * P], actg[:, t, b * P:(b + 1) * P], ident)
                    m.then_inc(f.T, 1)

            def down(f, tiles, step, g, slot, half, first, last):
                pe.wait_ge(lo_ready, g + 1)
                for t in range(tiles):
                    pe.wait_ge(f.lo, step * tiles + t + 1)
                    for kk in range(2):
                        for c in range(2):
                            whb, wlb = block_of(slot, 2 * kk + c)
                            b = 2 * half + kk
                            m = mm3(bank[4 + 2 * t + c][:], actThi[:, t, b, :], actTlo[:, t, b, :], whb, wlb,
                                    first and half == 0 and kk == 0, last and half == 1 and kk == 1)
                m.then_inc(w_used, 1)

            def swiglu(f, tiles, lhi, llo, base, slot0, n7, after_gate0=None, before_last=None, y_free=None):
                def s(i):
                    return (slot0 + i) % SPL
                pe_gate = lambda g, i, half: gate_up(f, tiles, lhi, llo, g, s(i), half, 0, f.gate)
                pe_up = lambda g, i, half: gate_up(f, tiles, lhi, llo, g, s(i), half, 2, f.up)
                pe_gate(base, 0, 0)
                pe_gate(base + 1, 1, 1)
                if after_gate0:
                    after_gate0()
                pe_up(base + 2, 2, 0)
                pe_up(base + 3, 3, 1)

                def body(j, first):
                    b = base + 4 + j * 6
                    pe.wait_ge(f.silu, (n7 + j + 1) * tiles)
                    pe_gate(b, 4, 0)
                    act_T(f, tiles, n7 + j)
                    pe_gate(b + 1, 5, 1)
                    down(f, tiles, n7 + j, b + 2, s(6), 0, first, False)
                    down(f, tiles, n7 + j, b + 3, s(7), 1, False, False)
                    pe_up(b + 4, 8, 0)
                    pe_up(b + 5, 9, 1)
                if y_free:
                    y_free()
                body(0, True)
                with pe.Fori(1, JF - 1) as j:
                    body(j, False)
                if before_last:
                    before_last()
                act_T(f, tiles, n7 + JF - 1)
                down(f, tiles, n7 + JF - 1, base + JOBG - 2, s(JOBG - 2), 0, False, False)
                down(f, tiles, n7 + JF - 1, base + JOBG - 1, s(JOBG - 1), 1, False, True)

            def dense():
                norm_T(2)
                pe.wait_ge(hTlo_s, 12)
                tok = lambda t: slice(t * P, (t + 1) * P)
                swiglu(dn, TT, lambda k, t: hThi[:, k, tok(t)], lambda k, t: hTlo[:, k, tok(t)],
                       dense_base, dense_base, 0, y_free=lambda: pe.wait_ge(x_s, 4))

            def gather():
                for k in range(KD):
                    for t in range(TT):
                        m = mm(bank[6 + k // 4][:, (k % 4) * P:(k % 4 + 1) * P], hs[:, t, k * P:(k + 1) * P],
                               selG[:, t, :], t == 0, t == TT - 1)
                    if k % 4 == 3:
                        m.then_inc(gth_s, 1)

            def scatter():
                for t in range(TT):
                    for c in range(2):
                        mm(bank[((1, 3), (6, 7))[t][c]][:], selS[:, t * P:(t + 1) * P], ysb[:, c * 512:(c + 1) * 512],
                           True, True).then_inc(sca_s, 1)

            def router():
                norm_T(5)
                pe.wait_ge(hTlo_s, 24)
                pe.wait_ge(wrl_s, 2)
                for k in range(KD):
                    for i, (a, b) in enumerate([(0, 0), (0, 1), (1, 0), (1, 1)]):
                        w = (actThi, actTlo)[a][:].rearrange("p t b s -> p (t b) s")[:, k, :]
                        m = mm(bank[4][:, 0:SEQ], w, (hThi, hTlo)[b][:, k, :], k == 0 and i == 0, k == KD - 1 and i == 3)
                m.then_inc(lg_s, 1)
                pe.wait_ge(lgc_s, 1)
                for t in range(TT):
                    m = nc.tensor.transpose(bank[5][:, t * NE:(t + 1) * NE], lgT[:, t * P:(t + 1) * P], ident[0:NE, 0:NE])
                m.then_inc(lt_s, 1)
                pe.wait_ge(d_s, 1)
                o = lambda i: bank[6][:, i * NE:(i + 1) * NE]
                mm(o(0), upper, both[:, 0, :], True, True)
                mm(o(1), upper, both[:, 1, :], True, False)
                mm(o(1), ones, both[:, 0, :], False, True)
                mm(o(2), ones, both[:, 0, :], True, False)
                mm(o(2), ones, both[:, 1, :], False, True).then_inc(cnt_s, 1)
                pe.wait_ge(diag_s, 8)
                for i in range(2):
                    mm(bank[2 + i][:], ones, diag[:, 4 * i:4 * i + 4, :], True, True).then_inc(row_s, 1)

            mix(0)
            dense()
            mix(1)
            router()
            pe.wait_ge(job_s, 1)
            njobs = pe.value_load(jobtab[0:1, MAXJ:MAXJ + 1], min_val=1, max_val=MAXJ)
            pe.wait_ge(sel_s, 1)
            gather()
            with pe.Fori(0, njobs) as n:
                pe.wait_ge(xlo_s, n * 2 + 2)

                def scatter_last():
                    pe.wait_ge(yc_s, n * 2 + 2)
                    pe.wait_ge(gst_s, n + 1)
                    scatter()

                def gather_next():
                    pe.wait_ge(sel_s, n + 2)
                    pe.wait_ge(xadd_s, n * 4 + 4)
                    gather()

                swiglu(mo, 1, lambda k, t: xThi[:, k, :], lambda k, t: xTlo[:, k, :],
                       n * JOBG + moe_base, moe_base, n * JF,
                       after_gate0=scatter_last,
                       before_last=gather_next)
            pe.wait_ge(yc_s, njobs * 2 + 2)
            pe.wait_ge(gst_s, njobs + 1)
            scatter()

        @block.scalar
        def _(act):
            def split_hi(g, off, lap):
                act.wait_ge(landed[off % RAW], (lap + 1) * 16)
                if not isinstance(g, int) or g >= SPL:
                    act.wait_ge(w_used, g - SPL + 1)
                nc.scalar.activation(whi[:, off % SPL, :], raw[:, off % RAW, :], ACT.Copy).then_inc(hi_ready, 1)

            def his(*gs):
                for g in gs:
                    split_hi(g, g, g // RAW)

            def norm_stats(u, width=D):
                if u == 0:
                    act.wait_ge(in_x, 32)
                    act.wait_ge(eps_set, 1)
                if x_need[u]:
                    act.wait_ge(x_s, x_need[u])
                if u:
                    act.wait_ge(hTp_s, 4 * u)
                for t in range(TT):
                    m = nc.scalar.activation(hs[:, t, :], xs[:, t, :], ACT.Square, accum_out=ss[:, t:t + 1])
                m.then_inc(sq_s, 1)
                v = {0: 1, 2: 2, 3: 3, 5: 4}[u]
                act.wait_ge(sq_s, v)
                nc.scalar.activation(ss, ss, ACT.Sqrt, bias=eps, scale=1.0 / D).then_inc(std_s, 1)

            def hT_hi(u):
                for b in range(4):
                    act.wait_ge(hTp_s, 4 * u + b + 1)
                    nc.scalar.activation(hThi[:, 2 * b:2 * b + 2, :].rearrange("p k s -> p (k s)"), bank[b][:],
                                         ACT.Copy).then_inc(hThi_s, 1)

            def copy(o, i, s):
                return nc.scalar.activation(o, i, ACT.Copy).then_inc(s, 1)

            def mix(l):
                b = mix_base[l]
                norm_stats(3 * l)
                his(b)
                hT_hi(3 * l)
                his(b + 1, b + 2, b + 3, b + 4)
                act.wait_ge(w_used, b + 2)
                for t in range(TT):
                    copy(zs[:, t, 0:512], bank[4 + t][:], zc_s)
                act.wait_ge(w_used, b + 4)
                for t in range(TT):
                    copy(zs[:, t, 512:1024], bank[6 + t][:], zc_s)
                act.wait_ge(w_used, b + 5)
                for t in range(TT):
                    copy(zs[:, t, 1024:DIN], bank[t][:, 0:256], zc_s)
                act.wait_ge(fA_s, l + 1)
                for i in range(2):
                    copy(fmixA[:, i, :], bank[2 + i][:], fAc_s)
                act.wait_ge(qss_s, l + 1)
                q = qss.rearrange("p a b -> p (a b)")
                nc.scalar.activation(q, q, ACT.Sqrt, bias=eps, scale=1.0 / HEAD).then_inc(qstd_s, 1)
                if l == 0:
                    act.wait_ge(trig_in, 2)
                    for o, i in ((sin, ang), (cos, ang2)):
                        nc.scalar.activation(o.rearrange("p a b -> p (a b)"), i.rearrange("p a b -> p (a b)"),
                                             ACT.Sin).then_inc(trig_s, 1)
                his(b + 5)
                for c in range(4):
                    act.wait_ge(pos_s, 4 * l + c + 1)
                    copy(posT[:, c, :], bank[4 + c][:], posc_s)
                for i in range(3):
                    act.wait_ge(qT_s, 3 * l + i + 1)
                    n = 2 if i < 2 else 1
                    copy(zs[:, :, 2 * i * P:(2 * i + n) * P].rearrange("p t (a c) -> p a t c", a=n),
                         bank[i][:, 0:n * SEQ].rearrange("p (a t c) -> p a t c", a=n, t=TT), qTc_s)
                his(b + 6, b + 7)
                for r in range(NKV):
                    act.wait_ge(mx_s, 2 * l + r + 1)
                    for i in range(QPK):
                        for t in range(TT):
                            nc.scalar.activation(probs[:, r, i, t, :], probs[:, r, i, t, :], ACT.Exp,
                                                 bias=negm[:, r, i, t:t + 1], scale=SCALE,
                                                 accum_out=rsum[:, r, i, t:t + 1]).then_inc(exp_s, 1)
                    es = esink[:, r].rearrange("p a b -> p (a b)")
                    nc.scalar.activation(es, es, ACT.Exp).then_inc(e_s, 1)
                    for i in range(2):
                        act.wait_ge(pT_s, 4 * (2 * l + r) + i + 1)
                        if r == 1 and i == 0:
                            act.wait_ge(o_s, 4 * l + 2)
                        copy(probsT[:, i].rearrange("p a b c -> p (a b c)"), bank[4 + i][:], pTa_s)
                for t in range(TT):
                    act.wait_ge(fo_s, 2 * l + t + 1)
                    copy(hs[:, t, DA:D], bank[t][:], foc_s)
                act.wait_ge(foc_s, 2 * l + 2)
                act.wait_ge(a_s, 4 * l + 4)
                for t in range(TT):
                    for c in range(2):
                        m = nc.scalar.activation(tflat[:, (2 * t + c) * 512:(2 * t + c + 1) * 512], hs[:, t, c * 512:(c + 1) * 512],
                                                 ACT.Square, accum_out=ssm[:, t, c:c + 1])
                m.then_inc(msq_s, 1)
                act.wait_ge(msq_s, l + 1)
                sm = ssm.rearrange("p a b -> p (a b)")
                nc.scalar.activation(sm, sm, ACT.Sqrt, bias=eps, scale=1.0 / DA).then_inc(mstd_s, 1)
                hT_hi(3 * l + 1)
                his(b + 8)

            def actT_hi(f, tiles, step):
                for t in range(tiles):
                    act.wait_ge(f.T, step * tiles + t + 1)
                    nc.scalar.activation(actThi[:, t].rearrange("p b s -> p (b s)"), bank[2 + t][:],
                                         ACT.Copy).then_inc(f.hi, 1)

            def swiglu(f, tiles, base, off0, lap0, n7, start=None, before_last=None):
                def sp_(i, extra=0):
                    split_hi(base + i + extra * 6, off0 + i, lap0 + (off0 % RAW + i) // RAW + extra)
                sp_(0)
                sp_(1)
                if start:
                    start()
                sp_(2)
                for t in range(tiles):
                    if t < tiles - 1:
                        act.wait_ge(f.gate, (n7 * (tiles - 1)) + t + 1)
                    else:
                        act.wait_ge(w_used, base + 2)
                    nc.scalar.activation(actg[:, t, :], bank[t][:], ACT.Silu).then_inc(f.silu, 1)
                sp_(3)
                sp_(4)
                sp_(5)
                with act.Fori(0, JF - 1) as j:
                    sp_(6, j)
                    actT_hi(f, tiles, n7 + j)
                    sp_(7, j)
                    for t in range(tiles):
                        if t < tiles - 1:
                            act.wait_ge(f.gate, (n7 + j + 1) * (tiles - 1) + t + 1)
                        else:
                            act.wait_ge(w_used, base + j * 6 + 6)
                        nc.scalar.activation(actg[:, t, :], bank[t][:], ACT.Silu).then_inc(f.silu, 1)
                    sp_(8, j)
                    sp_(9, j)
                    sp_(10, j)
                    sp_(11, j)
                if before_last:
                    before_last()
                actT_hi(f, tiles, n7 + JF - 1)

            mix(0)
            norm_stats(2)
            hT_hi(2)
            swiglu(dn, TT, dense_base, dense_base, dense_base // RAW, 0)
            mix(1)
            norm_stats(5)
            hT_hi(5)
            act.wait_ge(in_wr, 16)
            act.wait_ge(wrz_s, 2)
            act.wait_ge(w_used, moe_base)
            nc.scalar.activation(actThi[:].rearrange("p t b s -> p (t b) s")[:, :, 0:NE], wr, ACT.Copy).then_inc(wrc_s, 1)
            act.wait_ge(lg_s, 1)
            copy(lgT, bank[4][0:NE, 0:SEQ], lgc_s)
            act.wait_ge(d_s, 1)
            nc.scalar.activation(e2, e1, ACT.Exp).then_inc(e_s, 1)
            for i in range(2):
                act.wait_ge(row_s, i + 1)
                copy(rows[:, 2 * i:2 * i + 2, :].rearrange("p a b -> p (a b)"), bank[2 + i][:], rowc_s)

            def x_hi(n):
                for i in range(2):
                    act.wait_ge(gth_s, n * 2 + i + 1)
                    nc.scalar.activation(xThi[:, 4 * i:4 * i + 4, :].rearrange("p k s -> p (k s)"), bank[6 + i][:],
                                         ACT.Copy).then_inc(xhi_s, 1)

            def y_copy():
                for c in range(2):
                    copy(ysb[:, c * 512:(c + 1) * 512], bank[4 + c][:], yc_s)

            act.wait_ge(job_s, 1)
            njobs = act.value_load(jobtab[0:1, MAXJ:MAXJ + 1], min_val=1, max_val=MAXJ)
            x_hi(0)
            act.wait_ge(yz_s, 2)
            with act.Fori(0, njobs) as n:
                def y_last():
                    act.wait_ge(w_used, n * JOBG + moe_base)
                    y_copy()
                swiglu(mo, 1, n * JOBG + moe_base, moe_base, n * (JOBG // RAW) + moe_base // RAW, n * JF,
                       start=y_last, before_last=lambda: x_hi(n + 1))
            act.wait_ge(w_used, njobs * JOBG + moe_base)
            y_copy()

        @block.vector
        def _(dve):
            steps = [0]
            base_v = [None]

            def link(ins):
                steps[0] += 1
                ins.then_inc(link_s, 1)
                dve.wait_ge(link_s, steps[0] if base_v[0] is None else base_v[0] + steps[0])

            def tt(o, a, b, op):
                return nc.vector.tensor_tensor(o, a, b, op)

            def split_lo(g, off):
                dve.wait_ge(hi_ready, g + 1)
                tt(wlo[:, off % SPL, :], raw[:, off % RAW, :], whi[:, off % SPL, :].bitcast(F32),
                   ALU.subtract).then_inc(lo_ready, 1)

            def los(*gs):
                for g in gs:
                    split_lo(g, g)

            def hT_lo(u):
                for b in range(4):
                    dve.wait_ge(hThi_s, 4 * u + b + 1)
                    tt(hTlo[:, 2 * b:2 * b + 2, :].rearrange("p k s -> p (k s)"), bank[b][:],
                       hThi[:, 2 * b:2 * b + 2, :].rearrange("p k s -> p (k s)").bitcast(F32),
                       ALU.subtract).then_inc(hTlo_s, 1)

            def norm(u):
                v = {0: 1, 2: 2, 3: 3, 5: 4}[u]
                dve.wait_ge(std_s, v)
                link(nc.vector.reciprocal(ss, ss))
                dve.wait_ge(in_gain, 16 * v)
                for t in range(TT):
                    nc.vector.scalar_tensor_tensor(out=hs[:, t, :], in0=xs[:, t, :], scalar=ss[:, t:t + 1],
                                                   in1=gain1[:], op0=ALU.mult, op1=ALU.mult).then_inc(h_s, 1)

            def add_x(banks, s_done):
                for t in range(TT):
                    for c in range(2):
                        xa = xs[:, t, c * 512:(c + 1) * 512]
                        tt(xa, bank[banks[t][c]][:], xa, ALU.add).then_inc(s_done, 1)

            def trig():
                dve.wait_ge(in_p, 16 * TT)
                dve.wait_ge(in_c, 16)
                link(nc.vector.tensor_copy(posf, posi[:]))
                fr = cst[:, C_FREQ:C_FREQ + HALF]
                for t in range(TT):
                    m = nc.vector.tensor_scalar(ang[:, t, :], fr, posf[:, t:t + 1], None, ALU.mult)
                link(m)
                a, a2 = (v.rearrange("p a b -> p (a b)") for v in (ang, ang2))
                link(nc.vector.tensor_scalar(a2, a, 1.0 / TWO_PI, ROUND, ALU.mult, ALU.add))
                link(nc.vector.tensor_scalar(a2, a2, ROUND, None, ALU.subtract))
                for part in (PI_1, PI_2, PI_3):
                    link(nc.vector.scalar_tensor_tensor(out=a, in0=a2, scalar=-part, in1=a, op0=ALU.mult, op1=ALU.add))
                link(nc.vector.tensor_scalar(a, a, PI_SAFE, -PI_SAFE, ALU.min, ALU.max))
                link(nc.vector.scalar_tensor_tensor(out=a2, in0=a, scalar=-1.0, in1=a, op0=ALU.mult, op1=ALU.max))
                nc.vector.tensor_scalar(a2, a2, -1.0, TWO_PI / 4, ALU.mult, ALU.add).then_inc(trig_in, 2)

            def qk_norm(l):
                dve.wait_ge(zc_s, 6 * l + 4)
                zqk = zs[:, :, 0:NH * HEAD]
                link(tt(qks, zqk, zqk, ALU.mult))
                nc.vector.tensor_reduce(qss, qks.rearrange("p t (h d) -> p t h d", h=NH), AX_X,
                                        ALU.add).then_inc(qss_s, 1)
                dve.wait_ge(qstd_s, l + 1)
                link(nc.vector.reciprocal(qss, qss))
                for t in range(TT):
                    z3 = zs[:, t, 0:NH * HEAD].rearrange("p (h d) -> p h d", h=NH)
                    m = tt(z3, z3, qss[:, t].unsqueeze(2).broadcast_to([P, NH, HEAD]), ALU.mult)
                link(m)
                dve.wait_ge(in_mix, 80 * (l + 1))
                for t in range(TT):
                    tt(qks[:, t, 0:DQ].rearrange("p (i g d) -> p g i d", i=QPK, g=NKV),
                       zs[:, t, 0:DQ].rearrange("p (g i d) -> p g i d", g=NKV, i=QPK),
                       qkgain[:, 0:NQ, :].rearrange("p (g i) d -> p g i d", g=NKV), ALU.mult)
                    m = tt(qks[:, t, DQ:V0].rearrange("p (h d) -> p h d", h=NKV),
                           zs[:, t, DQ:V0].rearrange("p (h d) -> p h d", h=NKV), qkgain[:, NQ:NH, :], ALU.mult)
                link(m)
                if l == 0:
                    dve.wait_ge(trig_s, 2)
                h4 = qks.rearrange("p t (h d) -> p t h d", h=NH)
                x1, x2 = h4[:, :, :, 0:HALF], h4[:, :, :, HALF:2 * HALF]
                cb, sb_ = (v.unsqueeze(2).broadcast_to([P, TT, NH, HALF]) for v in (cos, sin))
                tt(rtmp[0], x1, cb, ALU.mult)
                tt(rtmp[1], x2, sb_, ALU.mult)
                tt(rtmp[2], x2, cb, ALU.mult)
                link(tt(rtmp[3], x1, sb_, ALU.mult))
                tt(x1, rtmp[0], rtmp[1], ALU.subtract)
                tt(x2, rtmp[2], rtmp[3], ALU.add).then_inc(qk_s, 1)

            def softmax(l, r):
                for i in range(QPK):
                    dve.wait_ge(sc_s, 8 * l + 4 * r + i + 1)
                    m = tt(probs[:, r, i].rearrange("p t s -> p (t s)"), bank[4 * (1 - r) + i][:], mask,
                           ALU.add).then_inc(scm_s, 1)
                dve.wait_ge(scm_s, 8 * l + 4 * r + 4)
                m3, n3 = mx[:, r], negm[:, r]
                link(nc.vector.tensor_reduce(m3, probs[:, r], AX_X, ALU.max))
                sk = sinks[:, QPK * r:QPK * (r + 1)].unsqueeze(2).broadcast_to([P, QPK, TT])
                link(nc.vector.scalar_tensor_tensor(out=m3, in0=m3, scalar=SCALE, in1=sk, op0=ALU.mult, op1=ALU.max))
                nc.vector.tensor_tensor(esink[:, r], sk, m3, ALU.subtract)
                nc.vector.tensor_scalar(n3, m3, -1.0, None, ALU.mult).then_inc(mx_s, 1)

            def probsT_dve(l, r):
                for i in range(2, 4):
                    dve.wait_ge(pT_s, 4 * (2 * l + r) + i + 1)
                    if r == 1:
                        dve.wait_ge(o_s, 4 * l + 2)
                    nc.vector.tensor_copy(probsT[:, i].rearrange("p a b c -> p (a b c)"),
                                          bank[4 + i][:]).then_inc(pTd_s, 1)

            def attn_out(l, r):
                dve.wait_ge(e_s, 2 * l + r + 1)
                rs, es = (v[:, r].rearrange("p a b -> p (a b)") for v in (rsum, esink))
                link(tt(rs, rs, es, ALU.add))
                link(nc.vector.reciprocal(rs, rs))
                for t in range(TT):
                    dve.wait_ge(o_s, 4 * l + 2 * r + t + 1)
                    tt(hs[:, t, r * 256:(r + 1) * 256].rearrange("p (h d) -> p h d", h=QPK),
                       bank[2 * r + t][:, 0:256].rearrange("p (h d) -> p h d", h=QPK),
                       rsum[:, r, :, t].unsqueeze(2).broadcast_to([P, QPK, HEAD]), ALU.mult).then_inc(a_s, 1)

            def mix(l):
                b = mix_base[l]
                norm(3 * l)
                los(b)
                hT_lo(3 * l)
                los(b + 1, b + 2, b + 3, b + 4)
                qk_norm(l)
                los(b + 5)
                los(b + 6, b + 7)
                softmax(l, 0)
                softmax(l, 1)
                probsT_dve(l, 0)
                attn_out(l, 0)
                probsT_dve(l, 1)
                attn_out(l, 1)
                dve.wait_ge(mstd_s, l + 1)
                link(nc.vector.reciprocal(ssm, ssm))
                dve.wait_ge(in_gain2, 32 * (l + 1))
                for t in range(TT):
                    for c in range(2):
                        hc = hs[:, t, c * 512:(c + 1) * 512]
                        m = nc.vector.scalar_tensor_tensor(out=hc, in0=hc, scalar=ssm[:, t, c:c + 1],
                                                           in1=gain2[:, c * 512:(c + 1) * 512], op0=ALU.mult, op1=ALU.mult)
                    m.then_inc(h_s, 1)
                hT_lo(3 * l + 1)
                los(b + 8)
                dve.wait_ge(w_used, b + 9)
                add_x(((4, 6), (5, 7)), x_s)

            def act_mul(f, tiles, step, granule_done):
                for t in range(tiles):
                    dve.wait_ge(f.silu, (step * tiles) + t + 1)
                    if t < tiles - 1:
                        dve.wait_ge(f.up, step * (tiles - 1) + t + 1)
                    else:
                        dve.wait_ge(w_used, granule_done)
                    tt(actg[:, t, :], bank[2 + t][:], actg[:, t, :], ALU.mult).then_inc(f.act, 1)

            def actT_lo(f, tiles, step):
                for t in range(tiles):
                    dve.wait_ge(f.hi, step * tiles + t + 1)
                    tt(actTlo[:, t].rearrange("p b s -> p (b s)"), bank[2 + t][:],
                       actThi[:, t].rearrange("p b s -> p (b s)").bitcast(F32), ALU.subtract).then_inc(f.lo, 1)

            def swiglu(f, tiles, base, off0, n7, start=None, middle=None, before_last=None):
                def sp_(i, extra=0):
                    split_lo(base + i + extra * 6, off0 + i)
                sp_(0)
                sp_(1)
                sp_(2)
                if start:
                    start()
                sp_(3)
                sp_(4)
                sp_(5)
                if middle:
                    middle()
                with dve.Fori(0, JF - 1) as j:
                    act_mul(f, tiles, n7 + j, base + j * 6 + 4)
                    sp_(6, j)
                    actT_lo(f, tiles, n7 + j)
                    sp_(7, j)
                    sp_(8, j)
                    sp_(9, j)
                    sp_(10, j)
                    sp_(11, j)
                act_mul(f, tiles, n7 + JF - 1, base + JOBG - 2)
                if before_last:
                    before_last()
                actT_lo(f, tiles, n7 + JF - 1)

            def router():
                a3 = lambda v: v.rearrange("p t b s -> p (t b) s")
                for v in (actThi, actTlo):
                    nc.vector.memset(a3(v[:]).bitcast(F32), 0.0).then_inc(wrz_s, 1)
                dve.wait_ge(wrc_s, 1)
                dve.wait_ge(wrz_s, 2)
                tt(a3(actTlo[:])[:, :, 0:NE], wr, a3(actThi[:])[:, :, 0:NE].bitcast(F32), ALU.subtract).then_inc(wrl_s, 2)
                dve.wait_ge(lt_s, 1)
                link(nc.vector.tensor_copy(lg.rearrange("p a b -> p (a b)"), bank[5][:, 0:TT * NE]))
                full = [P, TT, NE, NE]
                other, own = lg.unsqueeze(2).broadcast_to(full), lg.unsqueeze(3).broadcast_to(full)
                for t in range(TT):
                    tt(cmp1[:, t], other[:, t], own[:, t], ALU.is_gt)
                    m = tt(cmp2[:, t], other[:, t], own[:, t], ALU.is_equal)
                link(m)
                for t in range(TT):
                    m = tt(cmp2[:, t], cmp2[:, t], ltri, ALU.mult)
                link(m)
                link(tt(cmp1, cmp1, cmp2, ALU.add))
                link(nc.vector.tensor_reduce(rank, cmp1, AX_X, ALU.add))
                for c in range(2):
                    m = nc.vector.tensor_scalar(pick[:, c], rank, float(c), None, ALU.is_equal)
                link(m)
                for c in range(2):
                    tt(pickv[:, c], pick[:, c], lg, ALU.mult)
                link(tt(both, pick[:, 0], pick[:, 1], ALU.add))
                link(nc.vector.tensor_reduce(lc, pickv, AX_X, ALU.add))
                nc.vector.tensor_tensor(e1, lc[:, 1], lc[:, 0], ALU.subtract).then_inc(d_s, 1)
                dve.wait_ge(e_s, 5)
                link(nc.vector.tensor_scalar(e1, e2, 1.0, None, ALU.add))
                link(nc.vector.reciprocal(gate[:, 0], e1))
                tt(gate[:, 1], gate[:, 0], e2, ALU.mult)
                dve.wait_ge(cnt_s, 1)
                link(nc.vector.tensor_copy(posc.rearrange("p a b -> p (a b)"), bank[6][:, 0:3 * NE]))
                nc.vector.tensor_scalar(jobs, posc[:, 2], 0.0, None, ALU.is_gt)
                link(nc.vector.tensor_scalar(jobs2, posc[:, 2], float(P), None, ALU.is_gt))
                link(tt(jobs, jobs, jobs2, ALU.add))
                link(tt(cmp1[:, 0], jobs.unsqueeze(1).broadcast_to([P, NE, NE]), ltri, ALU.mult))
                link(nc.vector.tensor_reduce(jbase, cmp1[:, 0], AX_X, ALU.add))
                link(tt(jend, jbase, jobs, ALU.add))
                for t in range(TT):
                    m = nc.vector.scalar_tensor_tensor(out=posc[:, t], in0=jbase, scalar=float(P), in1=posc[:, t],
                                                       op0=ALU.mult, op1=ALU.add)
                link(m)
                for c in range(2):
                    m = tt(pickv[:, c], pick[:, c], posc[:, 0:TT], ALU.mult)
                link(m)
                link(nc.vector.tensor_reduce(gslot, pickv, AX_X, ALU.add))
                je = pflat[:, 3072:3200].rearrange("p (j e) -> p j e", j=MAXJ)
                link(tt(je, jend.unsqueeze(1).broadcast_to([P, MAXJ, NE]),
                        cst[:, C_JOB:C_JOB + MAXJ].unsqueeze(2).broadcast_to([P, MAXJ, NE]), ALU.is_le))
                link(nc.vector.tensor_reduce(jexp[:, 0:MAXJ], je, AX_X, ALU.add))
                nc.vector.tensor_copy(jexp[:, MAXJ:MAXJ + 1], jend[:, NE - 1:NE])
                link(nc.vector.tensor_scalar(jexp[:, 0:MAXJ], jexp[:, 0:MAXJ], NE - 1.0, None, ALU.min))
                nc.vector.tensor_copy(jobtab[:], jexp[0:1, :]).then_inc(job_s, 1)
                for q, v in enumerate((gslot, gate)):
                    for c in range(2):
                        for t in range(TT):
                            nc.vector.tensor_scalar(diag[:, 4 * q + 2 * c + t, :], ident, v[:, c, t:t + 1], None,
                                                    ALU.mult).then_inc(diag_s, 1)

            def select_tokens():
                for t in range(TT):
                    m = nc.vector.tensor_scalar(tmpS[:, t * P:(t + 1) * P], iota, gslot[:, 0, t:t + 1], None, ALU.is_equal)
                link(m)
                for t in range(TT):
                    m = nc.vector.scalar_tensor_tensor(out=selG[:, t, :], in0=iota, scalar=gslot[:, 1, t:t + 1],
                                                       in1=tmpS[:, t * P:(t + 1) * P], op0=ALU.is_equal, op1=ALU.add)
                m.then_inc(sel_s, 1)

            def select_slots():
                for c in range(2):
                    m = nc.vector.scalar_tensor_tensor(out=(tmpS, selS)[c], in0=rows[:, c, :], scalar=sidx,
                                                       in1=rows[:, 2 + c, :], op0=ALU.is_equal, op1=ALU.mult)
                link(m)
                tt(selS, selS, tmpS, ALU.add).then_inc(gst_s, 1)

            def x_lo(n):
                for i in range(2):
                    dve.wait_ge(xhi_s, n * 2 + i + 1)
                    tt(xTlo[:, 4 * i:4 * i + 4, :].rearrange("p k s -> p (k s)"), bank[6 + i][:],
                       xThi[:, 4 * i:4 * i + 4, :].rearrange("p k s -> p (k s)").bitcast(F32),
                       ALU.subtract).then_inc(xlo_s, 1)

            trig()
            mix(0)
            norm(2)
            hT_lo(2)
            swiglu(dn, TT, dense_base, dense_base, 0)
            dve.wait_ge(w_used, dense_base + JOBG)
            add_x(((4, 5), (6, 7)), x_s)
            mix(1)
            norm(5)
            hT_lo(5)
            router()
            for c in range(2):
                nc.vector.memset(bank[4 + c][:], 0.0).then_inc(yz_s, 1)
            dve.wait_ge(row_s, 2)
            nc.vector.memset(selS, 0.0).then_inc(gst_s, 1)
            nc.vector.tensor_copy(sidx, cst[:, C_PIDX:C_PIDX + 1])
            link(nc.vector.tensor_copy(iota, cst[:, C_IOTA:C_IOTA + P]))
            select_tokens()
            dve.wait_ge(rowc_s, 2)
            x_lo(0)
            dve.wait_ge(job_s, 1)
            njobs = dve.value_load(jobtab[0:1, MAXJ:MAXJ + 1], min_val=1, max_val=MAXJ)
            before = steps[0]
            STEPS = 3
            with dve.Fori(0, njobs) as n:
                base_v[0] = n * STEPS

                def scattered():
                    for t in range(TT):
                        for c in range(2):
                            dve.wait_ge(sca_s, n * 4 + 2 * t + c + 1)
                            xa = xs[:, t, c * 512:(c + 1) * 512]
                            tt(xa, bank[((1, 3), (6, 7))[t][c]][:], xa, ALU.add).then_inc(xadd_s, 1)

                def selections():
                    select_slots()
                    nc.vector.tensor_scalar(sidx, sidx, float(P), None, ALU.add)
                    link(nc.vector.tensor_scalar(iota, iota, float(P), None, ALU.add))
                    select_tokens()
                swiglu(mo, 1, n * JOBG + moe_base, moe_base, n * JF, start=scattered, middle=selections,
                       before_last=lambda: x_lo(n + 1))
                assert steps[0] == before + STEPS
            for t in range(TT):
                for c in range(2):
                    dve.wait_ge(sca_s, njobs * 4 + 2 * t + c + 1)
                    xa = xs[:, t, c * 512:(c + 1) * 512]
                    tt(xa, bank[((1, 3), (6, 7))[t][c]][:], xa, ALU.add).then_inc(xadd_s, 1)


def constants():
    import numpy as np

    c = np.zeros((P, C_N), np.float32)
    p = np.arange(P)
    c[:, C_ID:C_ID + P] = np.eye(P)
    q = np.arange(SEQ).reshape(TT, P).T[:, :, None]
    c[:, C_MASK:C_MASK + TT * SEQ] = np.where(np.abs(np.arange(SEQ) - q) <= 128, 0.0, -3e38).reshape(P, -1)
    a = 2 * np.pi * ((q * np.arange(SEQ)) % SEQ) / SEQ
    c[:, C_CS:C_CS + TT * 2 * SEQ] = np.concatenate([np.cos(a), np.sin(a)], -1).reshape(P, -1)
    b = np.arange(HEAD)
    b = 2 * np.pi * ((b[:, None] * b) % HEAD) / HEAD
    norm = 1.0 / np.sqrt(SEQ * HEAD)
    for i in range(2):
        r = slice(HEAD * i, HEAD * (i + 1))
        c[r, C_CC + HEAD * i:C_CC + HEAD * (i + 1)] = np.cos(b) * norm
        c[r, C_SC + HEAD * i:C_SC + HEAD * (i + 1)] = -np.sin(b) * norm
    c[:, C_U:C_U + P] = p[:, None] < p
    c[:, C_ONE:C_ONE + P] = 1.0
    c[:, C_IOTA:C_IOTA + P] = p
    e = np.arange(NE)
    c[:, C_LT:C_LT + NE * NE] = (e < e[:, None]).reshape(-1)
    c[:, C_FREQ:C_FREQ + HALF] = np.float32(500000.0) ** (-np.arange(0, 16, 2, dtype=np.float32) / np.float32(16))
    c[:, C_JOB:C_JOB + MAXJ] = np.arange(MAXJ)
    c[:, C_PIDX] = p
    return c


_INS = ['x', 'positions', 'norm_mix', 'w_in', 'q_norm', 'k_norm', 'sink', 'w_fmix', 'g_attn_out',
        'g_fourier_out', 'w_out', 'norm_ffn', 'ffn_gate', 'ffn_up', 'ffn_down', 'w_router',
        'e_gate', 'e_up', 'e_down']


def kernel(**inputs):
    import numpy as _np
    import concourse.bacc as _bacc
    from concourse.bass_utils import run_bass_kernel_spmd as _run

    nc = _bacc.Bacc("TRN2", target_bir_lowering=False, num_devices=1)
    arrays, args = {}, []
    for name, a in [(n, inputs[n]) for n in _INS] + [("consts", constants())]:
        a = _np.ascontiguousarray(a)
        arrays[f"in_{name}_dram"] = a
        args.append(nc.dram_tensor(f"in_{name}_dram", a.shape, mybir.dt.from_np(a.dtype), kind="ExternalInput").ap())
    args.append(nc.dram_tensor("out_0_dram", (1, SEQ, D), F32, kind="ExternalOutput").ap())
    build_trunk(nc, *args)
    r = _run(nc, [arrays], core_ids=[0])
    return r.results[0]["out_0_dram"]
```

```python
from contextlib import ExitStack

import concourse.bass as bass
from concourse import mybir

F32 = mybir.dt.float32
F32R = mybir.dt.float32r
I32 = mybir.dt.int32
ALU = mybir.AluOpType
ACT = mybir.ActivationFunctionType
AX_X = mybir.AxisListType.X

P = 128
SEQ, D, DEPTH = 256, 1024, 2
TT = SEQ // P
KD = D // P
HEAD, NQ, NKV = 64, 8, 2
QPK = NQ // NKV
DQ, DKV = NQ * HEAD, NKV * HEAD
DA = DF = D // 2
NH = NQ + NKV
DIN = DQ + 2 * DKV + DF
V0, FO0 = DQ + DKV, DQ + 2 * DKV
HALF = 8
FF, NE = 3584, 8
JF = FF // 512
EPS = 1e-6
SCALE = HEAD ** -0.5
SLOTS = 2 * P

GW = 2048
AHEAD = 2
RAW, SPL = 6, 3
MIXG = 9
JOBG = 6 * JF

C_ID = 0
C_MASK = C_ID + P
C_CS = C_MASK + TT * SEQ
C_CC = C_CS + TT * 2 * SEQ
C_SC = C_CC + P
C_U = C_SC + P
C_ONE = C_U + P
C_IOTA = C_ONE + P
C_LT = C_IOTA + P
C_FREQ = C_LT + NE * NE
C_JOB = C_FREQ + HALF
C_PIDX = C_JOB + NE
C_THR = C_PIDX + 1
C_N = C_THR + NE

TWO_PI = 6.283185307179586
PI_1 = 6.28125
PI_2 = 0.0019350051879882812
PI_3 = TWO_PI - PI_1 - PI_2
ROUND = 12582912.0
PI_SAFE = 3.1415925


def build_trunk(nc, x, positions, norm_mix, w_in, q_norm, k_norm, sink, w_fmix, g_attn_out,
                g_fourier_out, w_out, norm_ffn, ffn_gate, ffn_up, ffn_down, w_router,
                e_gate, e_up, e_down, consts, out):
    with ExitStack() as ctx:
        def sb(name, shape, dt=F32):
            return ctx.enter_context(nc.sbuf_tensor(name, shape, dt))

        def sem(name):
            return ctx.enter_context(nc.semaphore(name))

        raw = sb("raw", [P, RAW, GW])
        whi = sb("whi", [P, SPL, GW], F32R)
        wlo = sb("wlo", [P, SPL, GW], F32R)
        xs = sb("xs", [P, TT, D])
        hs = sb("hs", [P, TT, D])
        hThi = sb("hThi", [P, KD, SEQ], F32R)
        hTlo = sb("hTlo", [P, KD, SEQ], F32R)
        zs = sb("zs", [P, TT, DIN])
        probs = sb("probs", [P, NKV, QPK, TT, SEQ])
        probsT = sb("probsT", [P, QPK, 2, TT, P])
        posT = sb("posT", [P, 4, 2 * SEQ])
        fmixA = sb("fmixA", [P, 2, DF])
        fmixW = sb("fmixW", [P, 4, P])
        cst = sb("cst", [P, C_N])
        gain1 = sb("gain1", [P, D])
        gain2 = sb("gain2", [P, D])
        qkgain = sb("qkgain", [P, NH, HEAD])
        sinks = sb("sinks", [P, NQ])
        actThi = sb("actThi", [P, TT, 4, P], F32R)
        actTlo = sb("actTlo", [P, TT, 4, P], F32R)
        small = sb("small", [P, 640])
        posi = sb("posi", [P, TT], I32)
        jobtab = sb("jobtab", [1, 3 * NE + 1], I32)

        pflat = probs[:].rearrange("p a b c d -> p (a b c d)")
        actg = pflat[:, 0:1024].rearrange("p (t f) -> p t f", t=TT)
        ysb = pflat[:, 1024:2048]
        rows = pflat[:, 2048:3072].rearrange("p (c s) -> p c s", c=4)
        selG = pflat[:, 3072:3328].rearrange("p (t s) -> p t s", t=TT)
        selS = pflat[:, 3328:3584]
        tmpS = pflat[:, 3584:3840]
        diag = pflat[:, 0:1024].rearrange("p (c s) -> p c s", c=8)
        cmp1 = pflat[:, 3072:3200].rearrange("p (t a b) -> p t a b", t=TT, a=NE)
        cmp2 = pflat[:, 3200:3328].rearrange("p (t a b) -> p t a b", t=TT, a=NE)
        lgT = pflat[0:NE, 3328:3584]
        iota = pflat[:, 3840:3968]
        zflat = zs[:].rearrange("p t n -> p (t n)")
        ysb2 = zflat[:, 0:1024]
        selS2 = zflat[:, 1024:1280]
        tmpS2 = zflat[:, 1280:1536]
        selG2 = zflat[:, 1536:1792].rearrange("p (t s) -> p t s", t=TT)
        iota2 = zflat[:, 1792:1920]
        sidx2 = zflat[:, 1920:1921]
        tflat = probsT[:].rearrange("p a b c d -> p (a b c d)")
        qks = tflat[:, 0:TT * NH * HEAD].rearrange("p (t n) -> p t n", t=TT)
        wr = posT[:].rearrange("p a b -> p (a b)")[:, 0:KD * NE].rearrange("p (k e) -> p k e", k=KD)
        xThi = hThi[:].rearrange("p k s -> p (k s)").rearrange("p (t k s) -> p t k s", t=TT, k=KD)
        xTlo = hTlo[:].rearrange("p k s -> p (k s)").rearrange("p (t k s) -> p t k s", t=TT, k=KD)

        at = [0]

        def cols(n, *dims):
            a = small[:, at[0]:at[0] + n]
            at[0] += n
            if len(dims) == 2:
                a = a.rearrange("p (a b) -> p a b", a=dims[0])
            if len(dims) == 3:
                a = a.rearrange("p (a b c) -> p a b c", a=dims[0], b=dims[1])
            return a

        eps = cols(1)
        warm = cols(1)
        ss = cols(TT)
        ssm = cols(2 * TT, TT, 2)
        cos = cols(TT * HALF, TT, HALF)
        sin = cols(TT * HALF, TT, HALF)
        ang = cols(TT * HALF, TT, HALF)
        ang2 = cols(TT * HALF, TT, HALF)
        posf = cols(TT)
        qss = cols(TT * NH, TT, NH)
        mx = cols(NKV * QPK * TT, NKV, QPK, TT)
        negm = cols(NKV * QPK * TT, NKV, QPK, TT)
        esink = cols(NKV * QPK * TT, NKV, QPK, TT)
        rsum = cols(NKV * QPK * TT, NKV, QPK, TT)
        lg = cols(TT * NE, TT, NE)
        rank = cols(TT * NE, TT, NE)
        pick = cols(2 * TT * NE, 2, TT, NE)
        pickv = cols(2 * TT * NE, 2, TT, NE)
        both = cols(TT * NE, TT, NE)
        lc = cols(2 * TT, 2, TT)
        e2 = cols(TT)
        e1 = cols(TT)
        gate = cols(2 * TT, 2, TT)
        gslot = cols(2 * TT, 2, TT)
        posc = cols(3 * NE, 3, NE)
        jobs = cols(NE)
        jbase = cols(NE)
        jend = cols(NE)
        jexp = cols(3 * NE + 1)
        big = cols(NE)
        sidx = cols(1)
        assert at[0] <= 640
        rtmp = [pflat[:, i * 160:(i + 1) * 160]
                .rearrange("p (t h d) -> p t h d", t=TT, h=NH) for i in range(4)]

        ident = cst[:, C_ID:C_ID + P]
        mask = cst[:, C_MASK:C_MASK + TT * SEQ]
        dft = cst[:, C_CS:C_CS + TT * 2 * SEQ].rearrange("p (t n) -> p t n", t=TT)
        ones = cst[:, C_ONE:C_ONE + P]
        upper = cst[:, C_U:C_U + P]
        ltri = cst[:, C_LT:C_LT + NE * NE].rearrange("p (a b) -> p a b", a=NE)

        bank = [ctx.enter_context(nc.psum_tensor(f"bank{i}", [P, 512], F32)) for i in range(8)]

        in_x, in_id, in_c, in_p, in_gain0, in_gain, in_mix, in_gain2, in_wr = (
            sem("x_loaded"), sem("identity_loaded"), sem("consts_loaded"), sem("positions_loaded"),
            sem("first_gain1_loaded"), sem("gain1_loaded"), sem("mix_params_loaded"), sem("gain2_loaded"), sem("router_loaded"))
        landed = [sem(f"granule_landed{i}") for i in range(RAW)]
        hi_ready, lo_ready, w_used = sem("w_hi_ready"), sem("w_lo_ready"), sem("w_used")
        link_s = sem("dve_step")
        eps_set, fmix_zero = sem("eps_set"), sem("fmixw_zeroed")
        sq_s, sqd_s, std_s, h_s = sem("squares"), sem("squares_dve"), sem("std"), sem("h_ready")
        hTp_s, hThi_s, hTlo_s = sem("hT_in_psum"), sem("hT_hi"), sem("hT_lo")
        zc_s = sem("z_copied")
        trig_in, trig_s = sem("trig_args"), sem("trig_ready")
        fA_s, fAc_s = sem("fmixA_in_psum"), sem("fmixA_copied")
        pos_s, posc_s = sem("posT_in_psum"), sem("posT_copied")
        qss_s, qstd_s, qk_s = sem("qk_squares"), sem("qk_std"), sem("qk_ready")
        qT_s, qTc_s = sem("qT_in_psum"), sem("qT_copied")
        sc_s, scm_s, mx_s, exp_s = sem("scores"), sem("scores_masked"), sem("row_max"), sem("exps")
        pT_s, pTa_s, pTd_s = sem("probsT_in_psum"), sem("probsT_copied_act"), sem("probsT_copied_dve")
        o_s, a_s = sem("pv_in_psum"), sem("attn_ready")
        fo_s, foc_s = sem("fourier_in_psum"), sem("fourier_copied")
        msq_s, mstd_s = sem("mixed_squares"), sem("mixed_std")
        wo_s, x_s = sem("branch_in_psum"), sem("x_updated")

        class Ffn:
            pass

        def ffn_sems(tag):
            f = Ffn()
            f.silu, f.act = sem(tag + "silu"), sem(tag + "act_ready")
            f.T, f.hi, f.lo = sem(tag + "actT_in_psum"), sem(tag + "actT_hi"), sem(tag + "actT_lo")
            return f

        dn, mo = ffn_sems("d_"), ffn_sems("m_")
        wrc_s, wrz_s, wrl_s = sem("router_hi"), sem("router_zeroed"), sem("router_lo")
        lg_s, lgc_s, lt_s = sem("logitsT_in_psum"), sem("logitsT_copied"), sem("logits_in_psum")
        d_s, e_s, cnt_s, diag_s, row_s, rowc_s = (
            sem("choices_and_gap"), sem("exp_of_sink_or_gap"), sem("counts_in_psum"), sem("diag_ready"),
            sem("rows_in_psum"), sem("rows_copied"))
        job_s = sem("jobs_ready")
        sel_s, gth_s, xhi_s, xlo_s = sem("sel_ready"), sem("gathered"), sem("job_x_hi"), sem("job_x_lo")
        gst_s, yc_s, sca_s, xadd_s = sem("gated_sel_ready"), sem("y_copied"), sem("scattered"), sem("x_added")
        yz_s = sem("y_zeroed")
        sel2_s, gth2_s, xhi2_s, xlo2_s = sem("sel2_ready"), sem("gathered2"), sem("job_x2_hi"), sem("job_x2_lo")
        gst2_s, yc2_s, sca2_s, xadd2_s, link2_s = (sem("gated_sel2_ready"), sem("y2_copied"), sem("scattered2"),
                                                   sem("x2_added"), sem("dve_step2"))
        y0_s = sem("dense_first_tile_done")
        out_s = sem("out_stored")

        def read_jobs(eng):
            eng.wait_ge(job_s, 1)
            return eng.value_load(jobtab[0:1, 3 * NE:3 * NE + 1], min_val=1, max_val=NE)

        def read_job(eng, n):
            return (eng.value_load(jobtab[0:1, bass.ds(n + NE, 1)], min_val=0, max_val=1),
                    eng.value_load(jobtab[0:1, bass.ds(n + 2 * NE, 1)], min_val=0, max_val=NE - 1))

        block = ctx.enter_context(nc.Block())

        mix_base = [0, MIXG + JOBG]
        dense_base = MIXG
        moe_base = 2 * MIXG + JOBG
        assert moe_base % RAW == 0 and MIXG % SPL == 0 and JOBG % RAW == 0

        @block.sync
        def _(sp):
            sp.dma_start(xs[:, 0, :], x[0, 0:P, :]).then_inc(in_x, 16)
            sp.dma_start(xs[:, 1, :], x[0, P:SEQ, :]).then_inc(in_x, 16)
            sp.dma_start(cst[:, 0:P], consts[:, 0:P]).then_inc(in_id, 16)

            def slot_free(g):
                sp.wait_ge(lo_ready, g - RAW + 1)

            def put(slot, src):
                dst = raw[:, slot, :]
                if len(src.shape) == 3:
                    dst = dst.rearrange("p (k f) -> p k f", k=src.shape[1])
                sp.dma_start(dst, src).then_inc(landed[slot], 16)

            def mix(l):
                b = mix_base[l]
                wi = w_in[l].rearrange("(k p) n -> p k n", p=P)
                wo = w_out[l].rearrange("(k p) n -> p k n", p=P)
                srcs = [wi[:, 4 * h:4 * h + 4, 512 * c:512 * c + 512] for c in range(2) for h in range(2)]
                srcs += [wi[:, :, 1024:DIN]]
                srcs += [wo[:, 4 * h:4 * h + 4, 512 * c:512 * c + 512] for c in range(2) for h in range(2)]
                for i, s in enumerate(srcs):
                    if b + i >= RAW:
                        slot_free(b + i)
                    put((b + i) % RAW, s)
                    if b + i == 1:
                        sp.dma_start(cst[:, P:C_N], consts[:, P:C_N]).then_inc(in_c, 16)

            def ffn(part, base, slot0, wg, wu, wd):
                def up_gran(w, j, h):
                    return w[:, 4 * h:4 * h + 4, bass.ds(j * 512, 512)]

                def down_gran(j, h):
                    return wd[:, bass.ds(j * 4 + 2 * h, 2), :]

                if part == "start":
                    for i, s in enumerate([up_gran(wg, 0, 0), up_gran(wg, 0, 1), up_gran(wu, 0, 0), up_gran(wu, 0, 1)]):
                        slot_free(base + i)
                        put((slot0 + i) % RAW, s)
                    return
                with sp.Fori(0, JF - 1) as j:
                    for c in range(6):
                        slot_free(base + 4 + j * 6 + c)
                        s = [up_gran(wg, j + 1, 0), up_gran(wg, j + 1, 1), down_gran(j, 0), down_gran(j, 1),
                             up_gran(wu, j + 1, 0), up_gran(wu, j + 1, 1)][c]
                        put((slot0 + 4 + c) % RAW, s)
                for h in range(2):
                    slot_free(base + JOBG - 2 + h)
                    put((slot0 + JOBG - 2 + h) % RAW, down_gran(JF - 1, h))

            mix(0)
            for part in ("start", "rest"):
                ffn(part, dense_base, dense_base, ffn_gate[0].rearrange("(k p) n -> p k n", p=P),
                    ffn_up[0].rearrange("(k p) n -> p k n", p=P), ffn_down[0].rearrange("(k p) n -> p k n", p=P))
            mix(1)

            def job(part, n, e):
                w = [w_[0].rearrange("e (k p) n -> e p k n", p=P)[bass.ds(e, 1)].rearrange("e p k n -> (e p) k n")
                     for w_ in (e_gate, e_up, e_down)]
                ffn(part, n * JOBG + moe_base, moe_base, *w)

            def expert_of(n):
                return sp.value_load(jobtab[0:1, bass.ds(n, 1)], min_val=0, max_val=NE - 1)

            job("start", 0, 0)
            njobs = read_jobs(sp)
            with sp.Fori(0, njobs - 1) as n:
                job("rest", n, expert_of(n))
                job("start", n + 1, expert_of(n + 1))
            job("rest", njobs - 1, expert_of(njobs - 1))
            for i in range(AHEAD):
                slot_free(njobs * JOBG + moe_base + i)
                put((moe_base + i) % RAW, e_gate[0, 0].rearrange("(k p) n -> p k n", p=P)[:, 0:4, 0:512])
            for t in range(TT):
                sp.wait_ge(xadd_s, njobs * 4 + 2 * t + 2)
                sp.dma_start(out[0, t * P:(t + 1) * P, :], xs[:, t, :]).then_inc(out_s, 16)
            sp.wait_ge(out_s, 16 * TT)

        @block.gpsimd
        def _(pool):
            nc.gpsimd.memset(eps, EPS).then_inc(eps_set, 1)
            nc.gpsimd.memset(fmixW[:], 0.0).then_inc(fmix_zero, 1)
            for t in range(TT):
                pool.dma_start(posi[:, t:t + 1],
                               positions[0, t * P:(t + 1) * P].rearrange("(p o) -> p o", o=1)).then_inc(in_p, 16)
            pool.wait_ge(fmix_zero, 1)

            def mix_params(l):
                pool.dma_start(qkgain[:, 0:NQ, :], q_norm[l].partition_broadcast(P).unsqueeze(1)
                               .broadcast_to([P, NQ, HEAD])).then_inc(in_mix, 16)
                pool.dma_start(qkgain[:, NQ:NH, :], k_norm[l].partition_broadcast(P).unsqueeze(1)
                               .broadcast_to([P, NKV, HEAD])).then_inc(in_mix, 16)
                pool.dma_start(sinks[:], sink[l].partition_broadcast(P)).then_inc(in_mix, 16)
                for a in range(2):
                    pool.dma_start(fmixW[64 * a:64 * a + 64, :, 64 * a:64 * a + 64],
                                   w_fmix[l].rearrange("(c two) i o -> two i c o", two=2)[a]).then_inc(in_mix, 16)

            def gain(g):
                pool.dma_start(gain1[:], g.partition_broadcast(P)).then_inc(in_gain, 16)

            def gains2(l):
                pool.dma_start(gain2[:, 0:DA], g_attn_out[l].partition_broadcast(P)).then_inc(in_gain2, 16)
                pool.dma_start(gain2[:, DA:D], g_fourier_out[l].partition_broadcast(P)).then_inc(in_gain2, 16)

            mix_params(0)
            gains2(0)
            pool.wait_ge(h_s, 2 * TT)
            gain(norm_ffn[0])
            pool.wait_ge(h_s, 4 * TT)
            mix_params(1)
            gains2(1)
            pool.wait_ge(h_s, 6 * TT)
            gain(norm_mix[1])
            pool.wait_ge(h_s, 8 * TT)
            gain(norm_ffn[1])
            pool.wait_ge(w_used, MIXG + JOBG)
            for v in (actThi, actTlo):
                nc.gpsimd.memset(v[:].bitcast(F32), 0.0).then_inc(wrz_s, 1)
            pool.wait_ge(mstd_s, 2)
            pool.dma_start(wr, w_router[0].rearrange("(k p) e -> p k e", p=P)).then_inc(in_wr, 16)

        x_need = {0: 0, 2: 4, 3: 8, 5: 12}

        @block.tensor
        def _(pe):
            def mm(o, a, b, start, stop):
                return nc.tensor.matmul(o, a, b, start=start, stop=stop)

            def mm3(o, ahi, alo, bhi, blo, start, stop):
                mm(o, ahi, bhi, start, False)
                mm(o, ahi, blo, False, False)
                return mm(o, alo, bhi, False, stop)

            def block_of(slot, b, width=512):
                return whi[:, slot, b * width:(b + 1) * width], wlo[:, slot, b * width:(b + 1) * width]

            def norm_T(u):
                if u:
                    pe.wait_ge(hTlo_s, 4 * u)
                else:
                    pe.wait_ge(in_id, 16)
                for t in range(TT):
                    for k in range(KD):
                        if k % 4 == 0:
                            pe.wait_ge(h_s, 2 * (u * TT + t) + k // 4 + 1)
                        m = nc.tensor.transpose(bank[k // 2][:, (k % 2) * SEQ + t * P:(k % 2) * SEQ + (t + 1) * P],
                                                hs[:, t, k * P:(k + 1) * P], ident)
                        if t == TT - 1 and k % 2:
                            m.then_inc(hTp_s, 1)

            def hT_split(u, k):
                if k % 2 == 0:
                    pe.wait_ge(hTlo_s, 4 * u + k // 2 + 1)

            def project(g, banks, first, last, u=None):
                pe.wait_ge(lo_ready, g + 1)
                for t in range(TT):
                    for b in range(4):
                        k = (0 if first else 4) + b
                        if u is not None and t == 0:
                            hT_split(u, k)
                        whb, wlb = block_of(g % SPL, b)
                        tok = slice(t * P, (t + 1) * P)
                        m = mm3(bank[banks[t]][:], hThi[:, k, tok], hTlo[:, k, tok], whb, wlb,
                                first and b == 0, last and b == 3)
                m.then_inc(w_used, 1)

            def mix(l):
                base = mix_base[l]
                norm_T(3 * l)
                project(base, (4, 5), True, False, 3 * l)
                project(base + 1, (4, 5), False, True, 3 * l)
                project(base + 2, (6, 7), True, False)
                project(base + 3, (6, 7), False, True)
                g = base + 4
                pe.wait_ge(lo_ready, g + 1)
                for t in range(TT):
                    for k in range(KD):
                        whb, wlb = block_of(g % SPL, k, 256)
                        tok = slice(t * P, (t + 1) * P)
                        m = mm3(bank[t][:, 0:256], hThi[:, k, tok], hTlo[:, k, tok], whb, wlb, k == 0, k == KD - 1)
                m.then_inc(w_used, 1)
                if l == 0:
                    pe.wait_ge(in_c, 16)
                pe.wait_ge(in_mix, 80 * (l + 1))
                fw = fmixW[:].rearrange("p a b -> p (a b)")
                mm(bank[2][:], cst[:, C_CC:C_CC + P], fw, True, True)
                mm(bank[3][:], cst[:, C_SC:C_SC + P], fw, True, True).then_inc(fA_s, 1)
                pe.wait_ge(zc_s, 6 * (l + 1))
                for c in range(4):
                    for t in range(TT):
                        m = mm(bank[4 + c][:], zs[:, t, FO0 + c * P:FO0 + (c + 1) * P], dft[:, t, :],
                               t == 0, t == TT - 1)
                    m.then_inc(pos_s, 1)
                pe.wait_ge(qk_s, l + 1)
                pe.wait_ge(fAc_s, 2 * (l + 1))
                for i in range(5):
                    for t in range(TT):
                        m = nc.tensor.transpose(bank[i // 2][:, (i % 2) * SEQ + t * P:(i % 2) * SEQ + (t + 1) * P],
                                                qks[:, t, i * P:(i + 1) * P], ident)
                    if i % 2 or i == 4:
                        m.then_inc(qT_s, 1)
                pe.wait_ge(posc_s, 4 * (l + 1))
                pe.wait_ge(qTc_s, 3 * (l + 1))
                for r in range(NKV):
                    for i in range(QPK):
                        for t in range(TT):
                            rows_ = slice(HEAD * r, HEAD * r + HEAD)
                            m = mm(bank[4 * (1 - r) + i][:, t * SEQ:(t + 1) * SEQ], zs[rows_, t, i * P:(i + 1) * P],
                                   zs[rows_, :, 4 * P:5 * P], True, True)
                        m.then_inc(sc_s, 1)
                pe.wait_ge(scm_s, 8 * l + 4)
                for t in range(TT):
                    for c in range(4):
                        mm(bank[6 + t][:, c * P:(c + 1) * P], posT[:, c, t * P:(t + 1) * P],
                           fmixA[:, 0, c * P:(c + 1) * P], True, False)
                        m = mm(bank[6 + t][:, c * P:(c + 1) * P], posT[:, c, SEQ + t * P:SEQ + (t + 1) * P],
                               fmixA[:, 1, c * P:(c + 1) * P], False, True)
                    m.then_inc(fo_s, 1)
                for r in range(NKV):
                    if r:
                        pe.wait_ge(pTa_s, 2 * (2 * l + r))
                        pe.wait_ge(pTd_s, 2 * (2 * l + r))
                    for i in range(QPK):
                        pe.wait_ge(exp_s, 8 * (2 * l + r) + 2 * i + 2)
                        if r == 0 and i >= 2:
                            pe.wait_ge(foc_s, 2 * l + i - 1)
                        for kt in range(2):
                            for t in range(TT):
                                m = nc.tensor.transpose(bank[4 + i][:, (kt * TT + t) * P:(kt * TT + t + 1) * P],
                                                        probs[:, r, i, t, kt * P:(kt + 1) * P], ident)
                        m.then_inc(pT_s, 1)
                    if r == 0:
                        pe.wait_ge(scm_s, 8 * l + 8)
                    pe.wait_ge(pTa_s, 2 * (2 * l + r + 1))
                    pe.wait_ge(pTd_s, 2 * (2 * l + r + 1))
                    for t in range(TT):
                        for i in range(QPK):
                            for kt in range(2):
                                m = mm(bank[2 * r + t][:, i * P:(i + 1) * P], probsT[:, i, kt, t, :],
                                       zs[:, kt, V0:V0 + DKV], kt == 0, kt == 1)
                        m.then_inc(o_s, 1)
                norm_T(3 * l + 1)
                project(base + 5, (4, 5), True, False, 3 * l + 1)
                project(base + 6, (4, 5), False, True, 3 * l + 1)
                project(base + 7, (6, 7), True, False)
                project(base + 8, (6, 7), False, True)

            def gate_up(tiles, lhi, llo, g, slot, half, to_bank, tokens=None):
                pe.wait_ge(lo_ready, g + 1)
                for t in range(tiles):
                    for b in range(4):
                        whb, wlb = block_of(slot, b)
                        if tokens and t == 0:
                            tokens(4 * half + b)
                        m = mm3(bank[to_bank + t][:], lhi(4 * half + b, t), llo(4 * half + b, t), whb, wlb,
                                half == 0 and b == 0, half == 1 and b == 3)
                m.then_inc(w_used, 1)

            def act_T(f, tiles, step):
                for t in range(tiles):
                    pe.wait_ge(f.act, step * 2 + (t + 1) * (2 // tiles))
                    for b in range(4):
                        m = nc.tensor.transpose(bank[2 + t][:, b * P:(b + 1) * P], actg[:, t, b * P:(b + 1) * P], ident)
                    m.then_inc(f.T, 2 // tiles)

            def down(f, tiles, step, g, slot, half, first, last):
                pe.wait_ge(lo_ready, g + 1)
                for t in range(tiles):
                    pe.wait_ge(f.lo, step * 2 + (t + 1) * (2 // tiles))
                    for kk in range(2):
                        for c in range(2):
                            whb, wlb = block_of(slot, 2 * kk + c)
                            b = 2 * half + kk
                            m = mm3(bank[4 + 2 * t + c][:], actThi[:, t, b, :], actTlo[:, t, b, :], whb, wlb,
                                    first and half == 0 and kk == 0, last and half == 1 and kk == 1)
                    if f is dn and t == 0 and last and half == 1:
                        m.then_inc(y0_s, 1)
                m.then_inc(w_used, 1)

            def swiglu(f, tiles, lhi, llo, base, slot0, n7, after_gate0=None, before_last=None, y_free=None,
                       tokens=None):
                def s(i):
                    return (slot0 + i) % SPL
                pe_gate = lambda g, i, half: gate_up(tiles, lhi, llo, g, s(i), half, 0)
                pe_up = lambda g, i, half: gate_up(tiles, lhi, llo, g, s(i), half, 2)
                for half in range(2):
                    gate_up(tiles, lhi, llo, base + half, s(half), half, 0, tokens)
                if after_gate0:
                    after_gate0()
                pe_up(base + 2, 2, 0)
                pe_up(base + 3, 3, 1)

                def body(j, first):
                    b = base + 4 + j * 6
                    pe.wait_ge(f.silu, (n7 + j + 1) * 2)
                    pe_gate(b, 4, 0)
                    act_T(f, tiles, n7 + j)
                    pe_gate(b + 1, 5, 1)
                    down(f, tiles, n7 + j, b + 2, s(6), 0, first, False)
                    down(f, tiles, n7 + j, b + 3, s(7), 1, False, False)
                    pe_up(b + 4, 8, 0)
                    pe_up(b + 5, 9, 1)
                if y_free:
                    y_free()
                body(0, True)
                with pe.Fori(1, JF - 1) as j:
                    body(j, False)
                if before_last:
                    before_last(0)
                act_T(f, tiles, n7 + JF - 1)
                if before_last:
                    before_last(1)
                down(f, tiles, n7 + JF - 1, base + JOBG - 2, s(JOBG - 2), 0, False, False)
                down(f, tiles, n7 + JF - 1, base + JOBG - 1, s(JOBG - 1), 1, False, True)

            def dense():
                norm_T(2)
                tok = lambda t: slice(t * P, (t + 1) * P)
                swiglu(dn, TT, lambda k, t: hThi[:, k, tok(t)], lambda k, t: hTlo[:, k, tok(t)],
                       dense_base, dense_base, 0, y_free=lambda: pe.wait_ge(x_s, 4),
                       tokens=lambda k: hT_split(2, k))

            def gather(half, sel, done):
                for k in range(4 * half, 4 * half + 4):
                    for t in range(TT):
                        m = mm(bank[half][:, (k % 4) * P:(k % 4 + 1) * P], hs[:, t, k * P:(k + 1) * P],
                               sel[:, t, :], t == 0, t == TT - 1)
                m.then_inc(done, 1)

            def scatter(sel, y, b0, done):
                for t in range(TT):
                    for c in range(2):
                        mm(bank[b0 + 2 * t + c][:], sel[:, t * P:(t + 1) * P], y[:, c * 512:(c + 1) * 512],
                           True, True).then_inc(done, 1)

            def router():
                norm_T(5)
                pe.wait_ge(wrl_s, 1)
                for k in range(KD):
                    hT_split(5, k)
                    for i, (a, b) in enumerate([(0, 0), (0, 1), (1, 0), (1, 1)]):
                        w = (actThi, actTlo)[a][:].rearrange("p t b s -> p (t b) s")[:, k, :]
                        m = mm(bank[4][:, 0:SEQ], w, (hThi, hTlo)[b][:, k, :], k == 0 and i == 0, k == KD - 1 and i == 3)
                m.then_inc(lg_s, 1)
                pe.wait_ge(lgc_s, 1)
                for t in range(TT):
                    m = nc.tensor.transpose(bank[5][:, t * NE:(t + 1) * NE], lgT[:, t * P:(t + 1) * P], ident[0:NE, 0:NE])
                m.then_inc(lt_s, 1)
                pe.wait_ge(d_s, 1)
                o = lambda i: bank[6][:, i * NE:(i + 1) * NE]
                mm(o(0), upper, both[:, 0, :], True, True)
                mm(o(1), upper, both[:, 1, :], True, False)
                mm(o(1), ones, both[:, 0, :], False, True)
                mm(o(2), ones, both[:, 0, :], True, False)
                mm(o(2), ones, both[:, 1, :], False, True).then_inc(cnt_s, 1)
                pe.wait_ge(sel_s, 1)
                for half in range(2):
                    gather(half, selG, gth_s)
                pe.wait_ge(diag_s, 8)
                for i in range(2):
                    mm(bank[2 + i][:], ones, diag[:, 4 * i:4 * i + 4, :], True, True).then_inc(row_s, 1)

            mix(0)
            dense()
            mix(1)
            router()
            njobs = read_jobs(pe)
            with pe.Fori(0, njobs) as n:
                two, before = read_job(pe, n)

                def scatter_last():
                    pe.wait_ge(yc_s, n * 2 + 2)
                    pe.wait_ge(gst_s, n + 1)
                    scatter(selS, ysb, 4, sca_s)

                def gather_next(half):
                    if half == 0:
                        pe.wait_ge(sel_s, n + 2)
                        pe.wait_ge(mo.silu, (n + 1) * 2 * JF)
                    gather(half, selG, gth_s)

                def job_split(k):
                    if k % 4 == 0:
                        pe.wait_ge(xlo_s, n * 2 + k // 4 + 1)

                def job(tiles):
                    swiglu(mo, tiles, lambda k, t: xThi[:, t, k, :], lambda k, t: xTlo[:, t, k, :],
                           n * JOBG + moe_base, moe_base, n * JF, after_gate0=scatter_last,
                           before_last=gather_next, y_free=lambda: pe.wait_ge(xadd_s, n * 4 + 4),
                           tokens=job_split)

                with pe.If(two == 1):
                    pe.wait_ge(xlo_s, n * 2 + 2)
                    pe.wait_ge(sel2_s, before + 1)
                    for half in range(2):
                        gather(half, selG2, gth2_s)
                    pe.wait_ge(xlo2_s, before * 2 + 2)
                    job(2)
                    pe.wait_ge(mo.lo, (n + 1) * 2 * JF)
                    pe.wait_ge(xlo_s, n * 2 + 4)
                    pe.wait_ge(yc2_s, before * 2 + 2)
                    pe.wait_ge(gst2_s, before + 1)
                    scatter(selS2, ysb2, 0, sca2_s)
                    pe.wait_ge(xadd2_s, before * 4 + 4)
                with pe.Else():
                    job(1)
            pe.wait_ge(yc_s, njobs * 2 + 2)
            pe.wait_ge(gst_s, njobs + 1)
            scatter(selS, ysb, 4, sca_s)

        @block.scalar
        def _(act):
            act.dma_start(gain1[:], norm_mix[0].partition_broadcast(P)).then_inc(in_gain0, 16)

            def split_hi(g, off, lap):
                act.wait_ge(landed[off % RAW], (lap + 1) * 16)
                if not isinstance(g, int) or g >= SPL:
                    act.wait_ge(w_used, g - SPL + 1)
                nc.scalar.activation(whi[:, off % SPL, :], raw[:, off % RAW, :], ACT.Copy).then_inc(hi_ready, 1)

            def his(*gs):
                for g in gs:
                    split_hi(g, g, g // RAW)

            def warm_sqrt():
                nc.scalar.activation(warm, eps, ACT.Sqrt)

            def norm_stats(u):
                v = {0: 1, 2: 2, 3: 3, 5: 4}[u]
                if u == 0:
                    act.wait_ge(eps_set, 1)
                    warm_sqrt()
                    act.wait_ge(in_x, 32)
                else:
                    warm_sqrt()
                    act.wait_ge(hTp_s, 4 * u)
                    act.wait_ge(x_s, x_need[u] - 1)
                nc.scalar.activation(hs[:, 0, :], xs[:, 0, :], ACT.Square, accum_out=ss[:, 0:1]).then_inc(sq_s, 1)
                act.wait_ge(sq_s, v)
                act.wait_ge(sqd_s, v)
                nc.scalar.activation(ss, ss, ACT.Sqrt, bias=eps, scale=1.0 / D).then_inc(std_s, 1)

            def hT_hi(u):
                for b in range(4):
                    act.wait_ge(hTp_s, 4 * u + b + 1)
                    nc.scalar.activation(hThi[:, 2 * b:2 * b + 2, :].rearrange("p k s -> p (k s)"), bank[b][:],
                                         ACT.Copy).then_inc(hThi_s, 1)

            def copy(o, i, s):
                return nc.scalar.activation(o, i, ACT.Copy).then_inc(s, 1)

            def mix(l):
                b = mix_base[l]
                norm_stats(3 * l)
                if l == 0:
                    his(b)
                hT_hi(3 * l)
                his(b + 1, b + 2, b + 3, b + 4)
                act.wait_ge(w_used, b + 2)
                for t in range(TT):
                    copy(zs[:, t, 0:512], bank[4 + t][:], zc_s)
                act.wait_ge(w_used, b + 4)
                for t in range(TT):
                    copy(zs[:, t, 512:1024], bank[6 + t][:], zc_s)
                act.wait_ge(w_used, b + 5)
                for t in range(TT):
                    copy(zs[:, t, 1024:DIN], bank[t][:, 0:256], zc_s)
                act.wait_ge(fA_s, l + 1)
                for i in range(2):
                    copy(fmixA[:, i, :], bank[2 + i][:], fAc_s)
                act.wait_ge(qss_s, l + 1)
                q = qss.rearrange("p a b -> p (a b)")
                nc.scalar.activation(q, q, ACT.Sqrt, bias=eps, scale=1.0 / HEAD).then_inc(qstd_s, 1)
                if l == 0:
                    act.wait_ge(trig_in, 2)
                    for o, i in ((sin, ang), (cos, ang2)):
                        nc.scalar.activation(o.rearrange("p a b -> p (a b)"), i.rearrange("p a b -> p (a b)"),
                                             ACT.Sin).then_inc(trig_s, 1)
                his(b + 5)
                for c in range(4):
                    act.wait_ge(pos_s, 4 * l + c + 1)
                    copy(posT[:, c, :], bank[4 + c][:], posc_s)
                for i in range(3):
                    act.wait_ge(qT_s, 3 * l + i + 1)
                    n = 2 if i < 2 else 1
                    copy(zs[:, :, 2 * i * P:(2 * i + n) * P].rearrange("p t (a c) -> p a t c", a=n),
                         bank[i][:, 0:n * SEQ].rearrange("p (a t c) -> p a t c", a=n, t=TT), qTc_s)
                his(b + 6, b + 7)
                for r in range(NKV):
                    act.wait_ge(mx_s, 2 * l + r + 1)
                    for i in range(QPK):
                        for t in range(TT):
                            nc.scalar.activation(probs[:, r, i, t, :], probs[:, r, i, t, :], ACT.Exp,
                                                 bias=negm[:, r, i, t:t + 1], scale=SCALE,
                                                 accum_out=rsum[:, r, i, t:t + 1]).then_inc(exp_s, 1)
                        if r == 0 and i == 1:
                            for t in range(TT):
                                act.wait_ge(fo_s, 2 * l + t + 1)
                                copy(hs[:, t, DA:D], bank[6 + t][:], foc_s)
                    es = esink[:, r].rearrange("p a b -> p (a b)")
                    nc.scalar.activation(es, es, ACT.Exp).then_inc(e_s, 1)
                    for i in range(2):
                        act.wait_ge(pT_s, 4 * (2 * l + r) + i + 1)
                        if r == 1 and i == 0:
                            act.wait_ge(o_s, 4 * l + 2)
                        copy(probsT[:, i].rearrange("p a b c -> p (a b c)"), bank[4 + i][:], pTa_s)
                warm_sqrt()
                act.wait_ge(foc_s, 2 * l + 2)
                for c in (1, 0):
                    for t in range(TT):
                        if c == 0:
                            act.wait_ge(a_s, 4 * l + 3 + t)
                        m = nc.scalar.activation(posT[:, 2 * c + t, :], hs[:, t, c * 512:(c + 1) * 512],
                                                 ACT.Square, accum_out=ssm[:, t, c:c + 1])
                m.then_inc(msq_s, 1)
                act.wait_ge(msq_s, l + 1)
                sm = ssm.rearrange("p a b -> p (a b)")
                nc.scalar.activation(sm, sm, ACT.Sqrt, bias=eps, scale=1.0 / DA).then_inc(mstd_s, 1)
                hT_hi(3 * l + 1)
                his(b + 8, b + 9)

            def actT_hi(f, tiles, step):
                for t in range(tiles):
                    act.wait_ge(f.T, step * 2 + (t + 1) * (2 // tiles))
                    nc.scalar.activation(actThi[:, t].rearrange("p b s -> p (b s)"), bank[2 + t][:],
                                         ACT.Copy).then_inc(f.hi, 2 // tiles)

            def swiglu(f, tiles, base, off0, lap0, n7, start=None, before_last=None, done=0):
                def sp_(i, extra=0):
                    split_hi(base + i + extra * 6, off0 + i, lap0 + (off0 % RAW + i) // RAW + extra)

                def silu(granules):
                    act.wait_ge(w_used, granules)
                    for t in range(tiles):
                        nc.scalar.activation(actg[:, t, :], bank[t][:], ACT.Silu).then_inc(f.silu, 2 // tiles)
                for i in range(done, 2):
                    sp_(i)
                if start:
                    start()
                sp_(2)
                silu(base + 2)
                sp_(3)
                sp_(4)
                sp_(5)
                with act.Fori(0, JF - 1) as j:
                    sp_(6, j)
                    actT_hi(f, tiles, n7 + j)
                    sp_(7, j)
                    silu(base + j * 6 + 6)
                    sp_(8, j)
                    sp_(9, j)
                    sp_(10, j)
                    sp_(11, j)
                if before_last:
                    sp_(JOBG - 12, 2)
                    before_last(0)
                actT_hi(f, tiles, n7 + JF - 1)
                if before_last:
                    before_last(1)
                    sp_(JOBG - 11, 2)

            mix(0)
            norm_stats(2)
            hT_hi(2)
            swiglu(dn, TT, dense_base, dense_base, dense_base // RAW, 0, done=1)
            his(mix_base[1])
            mix(1)
            act.wait_ge(in_wr, 16)
            act.wait_ge(wrz_s, 2)
            nc.scalar.activation(actThi[:].rearrange("p t b s -> p (t b) s")[:, :, 0:NE], wr, ACT.Copy).then_inc(wrc_s, 1)
            norm_stats(5)
            hT_hi(5)
            act.wait_ge(lg_s, 1)
            copy(lgT, bank[4][0:NE, 0:SEQ], lgc_s)
            act.wait_ge(d_s, 1)
            nc.scalar.activation(e2, e1, ACT.Exp).then_inc(e_s, 1)
            his(moe_base + 1)
            def x_hi(n, half, tile=0, gathered=gth_s, done=xhi_s):
                act.wait_ge(gathered, n * 2 + half + 1)
                nc.scalar.activation(xThi[:, tile, 4 * half:4 * half + 4, :].rearrange("p k s -> p (k s)"),
                                     bank[half][:], ACT.Copy).then_inc(done, 1)

            def y_copy(y, b0, done):
                for c in range(2):
                    copy(y[:, c * 512:(c + 1) * 512], bank[b0 + c][:], done)

            for half in range(2):
                x_hi(0, half)
            for i in range(2):
                act.wait_ge(row_s, i + 1)
                copy(rows[:, 2 * i:2 * i + 2, :].rearrange("p a b -> p (a b)"), bank[2 + i][:], rowc_s)
            njobs = read_jobs(act)
            act.wait_ge(yz_s, 2)
            with act.Fori(0, njobs) as n:
                two, before = read_job(act, n)

                nc.scalar.activation(warm, eps, ACT.Silu)

                def y_last():
                    act.wait_ge(w_used, n * JOBG + moe_base)
                    y_copy(ysb, 4, yc_s)

                def job(tiles):
                    swiglu(mo, tiles, n * JOBG + moe_base, moe_base, n * (JOBG // RAW) + moe_base // RAW, n * JF,
                           start=y_last, before_last=lambda half: x_hi(n + 1, half), done=AHEAD)

                with act.If(two == 1):
                    for half in range(2):
                        x_hi(before, half, 1, gth2_s, xhi2_s)
                    job(2)
                    act.wait_ge(w_used, n * JOBG + moe_base + JOBG)
                    y_copy(ysb2, 6, yc2_s)
                with act.Else():
                    job(1)
            act.wait_ge(w_used, njobs * JOBG + moe_base)
            y_copy(ysb, 4, yc_s)

        @block.vector
        def _(dve):
            steps = [0]
            base_v = [None]

            def link(ins):
                steps[0] += 1
                ins.then_inc(link_s, 1)
                dve.wait_ge(link_s, steps[0] if base_v[0] is None else base_v[0] + steps[0])

            def tt(o, a, b, op):
                return nc.vector.tensor_tensor(o, a, b, op)

            def split_lo(g, off):
                dve.wait_ge(hi_ready, g + 1)
                tt(wlo[:, off % SPL, :], raw[:, off % RAW, :], whi[:, off % SPL, :].bitcast(F32),
                   ALU.subtract).then_inc(lo_ready, 1)

            def los(*gs):
                for g in gs:
                    split_lo(g, g)

            def hT_lo(u):
                for b in range(4):
                    dve.wait_ge(hThi_s, 4 * u + b + 1)
                    tt(hTlo[:, 2 * b:2 * b + 2, :].rearrange("p k s -> p (k s)"), bank[b][:],
                       hThi[:, 2 * b:2 * b + 2, :].rearrange("p k s -> p (k s)").bitcast(F32),
                       ALU.subtract).then_inc(hTlo_s, 1)

            def norm(u):
                v = {0: 1, 2: 2, 3: 3, 5: 4}[u]
                if u == 0:
                    dve.wait_ge(in_x, 32)
                else:
                    dve.wait_ge(hTp_s, 4 * u)
                    dve.wait_ge(x_s, x_need[u])
                nc.vector.tensor_tensor_reduce(out=hs[:, 1, :], in0=xs[:, 1, :], in1=xs[:, 1, :], scale=1.0, scalar=0.0,
                                               op0=ALU.mult, op1=ALU.add, accum_out=ss[:, 1:2]).then_inc(sqd_s, 1)
                dve.wait_ge(std_s, v)
                link(nc.vector.reciprocal(ss, ss))
                if u == 0:
                    dve.wait_ge(in_gain0, 16)
                else:
                    dve.wait_ge(in_gain, 16 * (v - 1))
                for t in range(TT):
                    for c in range(2):
                        cut = slice(c * 512, (c + 1) * 512)
                        nc.vector.scalar_tensor_tensor(out=hs[:, t, cut], in0=xs[:, t, cut], scalar=ss[:, t:t + 1],
                                                       in1=gain1[:, cut], op0=ALU.mult, op1=ALU.mult).then_inc(h_s, 1)

            def add_x(b, t, c, s_done):
                xa = xs[:, t, c * 512:(c + 1) * 512]
                tt(xa, bank[b][:], xa, ALU.add).then_inc(s_done, 1)

            def trig():
                dve.wait_ge(in_p, 16 * TT)
                dve.wait_ge(in_c, 16)
                link(nc.vector.tensor_copy(posf, posi[:]))
                fr = cst[:, C_FREQ:C_FREQ + HALF]
                for t in range(TT):
                    m = nc.vector.tensor_scalar(ang[:, t, :], fr, posf[:, t:t + 1], None, ALU.mult)
                link(m)
                a, a2 = (v.rearrange("p a b -> p (a b)") for v in (ang, ang2))
                link(nc.vector.tensor_scalar(a2, a, 1.0 / TWO_PI, ROUND, ALU.mult, ALU.add))
                link(nc.vector.tensor_scalar(a2, a2, ROUND, None, ALU.subtract))
                for part in (PI_1, PI_2, PI_3):
                    link(nc.vector.scalar_tensor_tensor(out=a, in0=a2, scalar=-part, in1=a, op0=ALU.mult, op1=ALU.add))
                link(nc.vector.tensor_scalar(a, a, PI_SAFE, -PI_SAFE, ALU.min, ALU.max))
                link(nc.vector.scalar_tensor_tensor(out=a2, in0=a, scalar=-1.0, in1=a, op0=ALU.mult, op1=ALU.max))
                nc.vector.tensor_scalar(a2, a2, -1.0, TWO_PI / 4, ALU.mult, ALU.add).then_inc(trig_in, 2)

            def qk_norm(l):
                dve.wait_ge(zc_s, 6 * l + 4)
                zqk = zs[:, :, 0:NH * HEAD]
                link(tt(qks, zqk, zqk, ALU.mult))
                nc.vector.tensor_reduce(qss, qks.rearrange("p t (h d) -> p t h d", h=NH), AX_X,
                                        ALU.add).then_inc(qss_s, 1)
                dve.wait_ge(qstd_s, l + 1)
                link(nc.vector.reciprocal(qss, qss))
                for t in range(TT):
                    z3 = zs[:, t, 0:NH * HEAD].rearrange("p (h d) -> p h d", h=NH)
                    m = tt(z3, z3, qss[:, t].unsqueeze(2).broadcast_to([P, NH, HEAD]), ALU.mult)
                link(m)
                dve.wait_ge(in_mix, 80 * (l + 1))
                for t in range(TT):
                    tt(qks[:, t, 0:DQ].rearrange("p (i g d) -> p g i d", i=QPK, g=NKV),
                       zs[:, t, 0:DQ].rearrange("p (g i d) -> p g i d", g=NKV, i=QPK),
                       qkgain[:, 0:NQ, :].rearrange("p (g i) d -> p g i d", g=NKV), ALU.mult)
                    m = tt(qks[:, t, DQ:V0].rearrange("p (h d) -> p h d", h=NKV),
                           zs[:, t, DQ:V0].rearrange("p (h d) -> p h d", h=NKV), qkgain[:, NQ:NH, :], ALU.mult)
                link(m)
                if l == 0:
                    dve.wait_ge(trig_s, 2)
                h4 = qks.rearrange("p t (h d) -> p t h d", h=NH)
                x1, x2 = h4[:, :, :, 0:HALF], h4[:, :, :, HALF:2 * HALF]
                cb, sb_ = (v.unsqueeze(2).broadcast_to([P, TT, NH, HALF]) for v in (cos, sin))
                tt(rtmp[0], x1, cb, ALU.mult)
                tt(rtmp[1], x2, sb_, ALU.mult)
                tt(rtmp[2], x2, cb, ALU.mult)
                link(tt(rtmp[3], x1, sb_, ALU.mult))
                tt(x1, rtmp[0], rtmp[1], ALU.subtract)
                tt(x2, rtmp[2], rtmp[3], ALU.add).then_inc(qk_s, 1)

            def softmax(l, r):
                for i in range(QPK):
                    dve.wait_ge(sc_s, 8 * l + 4 * r + i + 1)
                    m = tt(probs[:, r, i].rearrange("p t s -> p (t s)"), bank[4 * (1 - r) + i][:], mask,
                           ALU.add).then_inc(scm_s, 1)
                dve.wait_ge(scm_s, 8 * l + 4 * r + 4)
                m3, n3 = mx[:, r], negm[:, r]
                link(nc.vector.tensor_reduce(m3, probs[:, r], AX_X, ALU.max))
                sk = sinks[:, QPK * r:QPK * (r + 1)].unsqueeze(2).broadcast_to([P, QPK, TT])
                link(nc.vector.scalar_tensor_tensor(out=m3, in0=m3, scalar=SCALE, in1=sk, op0=ALU.mult, op1=ALU.max))
                nc.vector.tensor_tensor(esink[:, r], sk, m3, ALU.subtract)
                nc.vector.tensor_scalar(n3, m3, -1.0, None, ALU.mult).then_inc(mx_s, 1)

            def probsT_dve(l, r):
                for i in range(2, 4):
                    dve.wait_ge(pT_s, 4 * (2 * l + r) + i + 1)
                    if r == 1:
                        dve.wait_ge(o_s, 4 * l + 2)
                    nc.vector.tensor_copy(probsT[:, i].rearrange("p a b c -> p (a b c)"),
                                          bank[4 + i][:]).then_inc(pTd_s, 1)

            def attn_out(l, r):
                dve.wait_ge(e_s, 2 * l + r + 1)
                rs, es = (v[:, r].rearrange("p a b -> p (a b)") for v in (rsum, esink))
                link(tt(rs, rs, es, ALU.add))
                link(nc.vector.reciprocal(rs, rs))
                for t in range(TT):
                    dve.wait_ge(o_s, 4 * l + 2 * r + t + 1)
                    tt(hs[:, t, r * 256:(r + 1) * 256].rearrange("p (h d) -> p h d", h=QPK),
                       bank[2 * r + t][:].rearrange("p (h g d) -> p h g d", h=QPK, g=NKV)[:, :, r, :],
                       rsum[:, r, :, t].unsqueeze(2).broadcast_to([P, QPK, HEAD]), ALU.mult).then_inc(a_s, 1)

            def mix(l):
                b = mix_base[l]
                norm(3 * l)
                if l == 0:
                    los(b)
                hT_lo(3 * l)
                if l == 0:
                    trig()
                los(b + 1, b + 2, b + 3, b + 4)
                qk_norm(l)
                los(b + 5)
                softmax(l, 0)
                softmax(l, 1)
                probsT_dve(l, 0)
                los(b + 6)
                attn_out(l, 0)
                probsT_dve(l, 1)
                attn_out(l, 1)
                los(b + 7)
                dve.wait_ge(mstd_s, l + 1)
                link(nc.vector.reciprocal(ssm, ssm))
                dve.wait_ge(in_gain2, 32 * (l + 1))
                for t in range(TT):
                    for c in range(2):
                        hc = hs[:, t, c * 512:(c + 1) * 512]
                        nc.vector.scalar_tensor_tensor(out=hc, in0=hc, scalar=ssm[:, t, c:c + 1],
                                                       in1=gain2[:, c * 512:(c + 1) * 512],
                                                       op0=ALU.mult, op1=ALU.mult).then_inc(h_s, 1)
                hT_lo(3 * l + 1)
                los(b + 8)
                for c in range(2):
                    if c:
                        los(b + 9)
                        if l == 1:
                            router_split()
                    dve.wait_ge(w_used, b + 7 + 2 * c)
                    for t in range(TT):
                        add_x(4 + 2 * c + t, t, c, x_s)

            def act_mul(f, tiles, step, granules):
                dve.wait_ge(w_used, granules)
                for t in range(tiles):
                    dve.wait_ge(f.silu, step * 2 + (t + 1) * (2 // tiles))
                    tt(actg[:, t, :], bank[2 + t][:], actg[:, t, :], ALU.mult).then_inc(f.act, 2 // tiles)

            def actT_lo(f, tiles, step):
                for t in range(tiles):
                    dve.wait_ge(f.hi, step * 2 + (t + 1) * (2 // tiles))
                    tt(actTlo[:, t].rearrange("p b s -> p (b s)"), bank[2 + t][:],
                       actThi[:, t].rearrange("p b s -> p (b s)").bitcast(F32), ALU.subtract).then_inc(f.lo, 2 // tiles)

            def swiglu(f, tiles, base, off0, n7, start=None, middle=None, before_last=None, done=0):
                def sp_(i, extra=0):
                    split_lo(base + i + extra * 6, off0 + i)

                def chunk(j, middle=(None, None)):
                    act_mul(f, tiles, n7 + j, base + j * 6 + 4)
                    sp_(6, j)
                    actT_lo(f, tiles, n7 + j)
                    sp_(7, j)
                    sp_(8, j)
                    if middle[0]:
                        middle[0]()
                    sp_(9, j)
                    sp_(10, j)
                    if middle[1]:
                        middle[1]()
                    sp_(11, j)
                for i in range(done, 3):
                    sp_(i)
                if start:
                    start(0)
                sp_(3)
                if start:
                    start(1)
                sp_(4)
                sp_(5)
                if middle:
                    chunk(0, middle)
                with dve.Fori(1 if middle else 0, JF - 1) as j:
                    chunk(j)
                act_mul(f, tiles, n7 + JF - 1, base + JOBG - 2)
                if before_last:
                    sp_(JOBG - 6, 1)
                    before_last(0)
                actT_lo(f, tiles, n7 + JF - 1)
                if before_last:
                    before_last(1)
                    sp_(JOBG - 5, 1)

            def router_split():
                a3 = lambda v: v.rearrange("p t b s -> p (t b) s")
                dve.wait_ge(wrc_s, 1)
                tt(a3(actTlo[:])[:, :, 0:NE], wr, a3(actThi[:])[:, :, 0:NE].bitcast(F32), ALU.subtract).then_inc(wrl_s, 1)

            def router():
                dve.wait_ge(lt_s, 1)
                link(nc.vector.tensor_copy(lg.rearrange("p a b -> p (a b)"), bank[5][:, 0:TT * NE]))
                full = [P, TT, NE, NE]
                other, own = lg.unsqueeze(2).broadcast_to(full), lg.unsqueeze(3).broadcast_to(full)
                for t in range(TT):
                    tt(cmp1[:, t], other[:, t], own[:, t], ALU.is_gt)
                    m = tt(cmp2[:, t], other[:, t], own[:, t], ALU.is_equal)
                link(m)
                for t in range(TT):
                    m = tt(cmp2[:, t], cmp2[:, t], ltri, ALU.mult)
                link(m)
                link(tt(cmp1, cmp1, cmp2, ALU.add))
                link(nc.vector.tensor_reduce(rank, cmp1, AX_X, ALU.add))
                for c in range(2):
                    m = nc.vector.tensor_scalar(pick[:, c], rank, float(c), None, ALU.is_equal)
                link(m)
                for c in range(2):
                    tt(pickv[:, c], pick[:, c], lg, ALU.mult)
                link(tt(both, pick[:, 0], pick[:, 1], ALU.add))
                link(nc.vector.tensor_reduce(lc, pickv, AX_X, ALU.add))
                nc.vector.tensor_tensor(e1, lc[:, 1], lc[:, 0], ALU.subtract).then_inc(d_s, 1)
                dve.wait_ge(e_s, 5)
                link(nc.vector.tensor_scalar(e1, e2, 1.0, None, ALU.add))
                link(nc.vector.reciprocal(gate[:, 0], e1))
                tt(gate[:, 1], gate[:, 0], e2, ALU.mult)
                nc.vector.memset(selS, 0.0).then_inc(gst_s, 1)
                nc.vector.tensor_copy(sidx, cst[:, C_PIDX:C_PIDX + 1])
                link(nc.vector.tensor_copy(iota, cst[:, C_IOTA:C_IOTA + P]))
                for c in range(2):
                    nc.vector.memset(bank[4 + c][:], 0.0).then_inc(yz_s, 1)
                dve.wait_ge(cnt_s, 1)
                link(nc.vector.tensor_copy(posc.rearrange("p a b -> p (a b)"), bank[6][:, 0:3 * NE]))
                tt(jobs, posc[:, 2], cst[:, C_THR:C_THR + NE], ALU.is_gt)
                link(nc.vector.tensor_scalar(big, posc[:, 2], float(P), None, ALU.is_gt))
                link(tt(cmp1[:, 0], jobs.unsqueeze(1).broadcast_to([P, NE, NE]), ltri, ALU.mult))
                link(nc.vector.tensor_reduce(jbase, cmp1[:, 0], AX_X, ALU.add))
                link(tt(jend, jbase, jobs, ALU.add))
                for t in range(TT):
                    m = nc.vector.scalar_tensor_tensor(out=posc[:, t], in0=jbase, scalar=float(SLOTS), in1=posc[:, t],
                                                       op0=ALU.mult, op1=ALU.add)
                link(m)
                for c in range(2):
                    m = tt(pickv[:, c], pick[:, c], posc[:, 0:TT], ALU.mult)
                link(m)
                link(nc.vector.tensor_reduce(gslot, pickv, AX_X, ALU.add))
                select_tokens(selG, tmpS, iota, sel_s, link)
                for q, v in enumerate((gslot, gate)):
                    for c in range(2):
                        for t in range(TT):
                            nc.vector.tensor_scalar(diag[:, 4 * q + 2 * c + t, :], ident, v[:, c, t:t + 1], None,
                                                    ALU.mult).then_inc(diag_s, 1)
                full8 = [P, NE, NE]
                je, jb, jc = (pflat[:, 1024 + 64 * i:1088 + 64 * i].rearrange("p (j e) -> p j e", j=NE) for i in range(3))
                jrow = cst[:, C_JOB:C_JOB + NE].unsqueeze(2).broadcast_to(full8)
                bigb = big.unsqueeze(1).broadcast_to(full8)
                tt(jb, jbase.unsqueeze(1).broadcast_to(full8), jrow, ALU.is_equal)
                link(tt(je, jend.unsqueeze(1).broadcast_to(full8), jrow, ALU.is_le))
                tt(jc, je, bigb, ALU.mult)
                link(tt(jb, jb, bigb, ALU.mult))
                for i, v in enumerate((je, jb, jc)):
                    nc.vector.tensor_reduce(jexp[:, i * NE:(i + 1) * NE], v, AX_X, ALU.add)
                link(nc.vector.tensor_copy(jexp[:, 3 * NE:3 * NE + 1], jend[:, NE - 1:NE]))
                link(nc.vector.tensor_scalar(jexp[:, 0:NE], jexp[:, 0:NE], NE - 1.0, None, ALU.min))
                nc.vector.tensor_copy(jobtab[:], jexp[0:1, :]).then_inc(job_s, 1)

            def select_tokens(to, tmp, io, done, step):
                for t in range(TT):
                    m = nc.vector.tensor_scalar(tmp[:, t * P:(t + 1) * P], io, gslot[:, 0, t:t + 1], None, ALU.is_equal)
                step(m)
                for t in range(TT):
                    m = nc.vector.scalar_tensor_tensor(out=to[:, t, :], in0=io, scalar=gslot[:, 1, t:t + 1],
                                                       in1=tmp[:, t * P:(t + 1) * P], op0=ALU.is_equal, op1=ALU.add)
                m.then_inc(done, 1)

            def select_slots(to, tmp, idx, done, step):
                for c in range(2):
                    m = nc.vector.scalar_tensor_tensor(out=(tmp, to)[c], in0=rows[:, c, :], scalar=idx,
                                                       in1=rows[:, 2 + c, :], op0=ALU.is_equal, op1=ALU.mult)
                step(m)
                tt(to, to, tmp, ALU.add).then_inc(done, 1)

            def x_lo(n, half, tile=0, split=xhi_s, done=xlo_s):
                dve.wait_ge(split, n * 2 + half + 1)
                cut = lambda v: v[:, tile, 4 * half:4 * half + 4, :].rearrange("p k s -> p (k s)")
                tt(cut(xTlo), bank[half][:], cut(xThi).bitcast(F32), ALU.subtract).then_inc(done, 1)

            mix(0)
            norm(2)
            hT_lo(2)
            swiglu(dn, TT, dense_base, dense_base, 0, done=1)
            los(mix_base[1])
            for t in range(TT):
                if t == 0:
                    dve.wait_ge(y0_s, 1)
                else:
                    dve.wait_ge(w_used, dense_base + JOBG)
                for c in range(2):
                    add_x(4 + 2 * t + c, t, c, x_s)
            mix(1)
            norm(5)
            hT_lo(5)
            router()
            for half in range(2):
                x_lo(0, half)
            los(moe_base + 1)
            dve.wait_ge(rowc_s, 2)
            njobs = read_jobs(dve)
            start_steps = steps[0]
            STEPS, STEPS2 = 3, 3
            with dve.Fori(0, njobs) as n:
                base_v[0] = n * STEPS
                two, before = read_job(dve, n)
                step2 = [0]

                def link2(ins):
                    step2[0] += 1
                    ins.then_inc(link2_s, 1)
                    dve.wait_ge(link2_s, before * STEPS2 + step2[0])

                def scattered(t):
                    for c in range(2):
                        dve.wait_ge(sca_s, n * 4 + 2 * t + c + 1)
                        add_x(4 + 2 * t + c, t, c, xadd_s)

                def way_back():
                    select_slots(selS, tmpS, sidx, gst_s, link)

                def next_way_in():
                    nc.vector.tensor_scalar(sidx, sidx, float(SLOTS), None, ALU.add)
                    link(nc.vector.tensor_scalar(iota, iota, float(SLOTS), None, ALU.add))
                    select_tokens(selG, tmpS, iota, sel_s, link)

                def job(tiles):
                    steps[0] = start_steps
                    swiglu(mo, tiles, n * JOBG + moe_base, moe_base, n * JF, start=scattered,
                           middle=(way_back, next_way_in), before_last=lambda half: x_lo(n + 1, half), done=AHEAD)
                    assert steps[0] == start_steps + STEPS

                with dve.If(two == 1):
                    nc.vector.tensor_scalar(sidx2, sidx, float(P), None, ALU.add)
                    link2(nc.vector.tensor_scalar(iota2, iota, float(P), None, ALU.add))
                    select_tokens(selG2, tmpS2, iota2, sel2_s, link2)
                    for half in range(2):
                        x_lo(before, half, 1, xhi2_s, xlo2_s)
                    job(2)
                    select_slots(selS2, tmpS2, sidx2, gst2_s, link2)
                    assert step2[0] == STEPS2
                    for t in range(TT):
                        for c in range(2):
                            dve.wait_ge(sca2_s, before * 4 + 2 * t + c + 1)
                            add_x(2 * t + c, t, c, xadd2_s)
                with dve.Else():
                    job(1)
            for t in range(TT):
                for c in range(2):
                    dve.wait_ge(sca_s, njobs * 4 + 2 * t + c + 1)
                    add_x(4 + 2 * t + c, t, c, xadd_s)


def constants():
    import numpy as np

    c = np.zeros((P, C_N), np.float32)
    p = np.arange(P)
    c[:, C_ID:C_ID + P] = np.eye(P)
    q = np.arange(SEQ).reshape(TT, P).T[:, :, None]
    c[:, C_MASK:C_MASK + TT * SEQ] = np.where(np.abs(np.arange(SEQ) - q) <= 128, 0.0, -3e38).reshape(P, -1)
    a = 2 * np.pi * ((q * np.arange(SEQ)) % SEQ) / SEQ
    c[:, C_CS:C_CS + TT * 2 * SEQ] = np.concatenate([np.cos(a), np.sin(a)], -1).reshape(P, -1)
    b = np.arange(HEAD)
    b = 2 * np.pi * ((b[:, None] * b) % HEAD) / HEAD
    norm = 1.0 / np.sqrt(SEQ * HEAD)
    for i in range(2):
        r = slice(HEAD * i, HEAD * (i + 1))
        c[r, C_CC + HEAD * i:C_CC + HEAD * (i + 1)] = np.cos(b) * norm
        c[r, C_SC + HEAD * i:C_SC + HEAD * (i + 1)] = -np.sin(b) * norm
    c[:, C_U:C_U + P] = p[:, None] < p
    c[:, C_ONE:C_ONE + P] = 1.0
    c[:, C_IOTA:C_IOTA + P] = p
    e = np.arange(NE)
    c[:, C_LT:C_LT + NE * NE] = (e < e[:, None]).reshape(-1)
    c[:, C_FREQ:C_FREQ + HALF] = np.float32(500000.0) ** (-np.arange(0, 16, 2, dtype=np.float32) / np.float32(16))
    c[:, C_JOB:C_JOB + NE] = e
    c[:, C_PIDX] = p
    c[:, C_THR] = -1.0
    return c


_INS = ['x', 'positions', 'norm_mix', 'w_in', 'q_norm', 'k_norm', 'sink', 'w_fmix', 'g_attn_out',
        'g_fourier_out', 'w_out', 'norm_ffn', 'ffn_gate', 'ffn_up', 'ffn_down', 'w_router',
        'e_gate', 'e_up', 'e_down']


def kernel(**inputs):
    import numpy as _np
    import concourse.bacc as _bacc
    from concourse.bass_utils import run_bass_kernel_spmd as _run

    nc = _bacc.Bacc("TRN2", target_bir_lowering=False, num_devices=1)
    arrays, args = {}, []
    for name, a in [(n, inputs[n]) for n in _INS] + [("consts", constants())]:
        a = _np.ascontiguousarray(a)
        arrays[f"in_{name}_dram"] = a
        args.append(nc.dram_tensor(f"in_{name}_dram", a.shape, mybir.dt.from_np(a.dtype), kind="ExternalInput").ap())
    args.append(nc.dram_tensor("out_0_dram", (1, SEQ, D), F32, kind="ExternalOutput").ap())
    build_trunk(nc, *args)
    r = _run(nc, [arrays], core_ids=[0])
    return r.results[0]["out_0_dram"]
```
